# Optimizing a Trainium2 kernel written in Bass

```python
import math
import jax, jax.numpy as jnp
from jax import lax
import numpy as np

D_MODEL = 1024
BATCH = 1
SEQ = 256
DEPTH = 2
DEC_BATCH = 8
DEC_SEQ = 8
PAST_LEN = 256
PAGE_SIZE = 128

N_RET_LAYERS = DEPTH // 2
N_MOBA_LAYERS = DEPTH - N_RET_LAYERS

RET_HEADS = 4
RET_DK = D_MODEL // RET_HEADS
RET_DV = 2 * RET_DK
RET_VW = RET_HEADS * RET_DV
RET_CHUNK = 128
ROPE_BASE = 10000.0

MOBA_HEADS = 8
MOBA_HD = D_MODEL // MOBA_HEADS
MOBA_W = MOBA_HEADS * MOBA_HD
MOBA_BLOCK = 256
MOBA_TOPK = 3
MOBA_Q_BLOCK = 64

REL_BUCKETS = 32
REL_MAX_DIST = 128
EPS = 1e-6

kernel_name = "yoco_retention_moba_step"

def rmsnorm(x, w):
    xf = x.astype(jnp.float32)
    y = xf * lax.rsqrt(jnp.mean(xf * xf, axis=-1, keepdims=True) + EPS)
    return (y * w.astype(jnp.float32)).astype(x.dtype)

def rotary(x, pos):
    half = x.shape[-1] // 2
    inv_freq = ROPE_BASE ** (-jnp.arange(half, dtype=jnp.float32) / half)
    ang = pos.astype(jnp.float32)[:, None] * inv_freq[None, :]
    cos = jnp.cos(ang)[None, :, None, :]
    sin = jnp.sin(ang)[None, :, None, :]
    xf = x.astype(jnp.float32)
    x1, x2 = xf[..., :half], xf[..., half:]
    return jnp.concatenate([x1 * cos - x2 * sin, x1 * sin + x2 * cos], axis=-1)

def ret_log_decay():
    return jnp.log1p(-jnp.exp2(-5.0 - jnp.arange(RET_HEADS, dtype=jnp.float32)))

def retention_chunk(S, q, k, v):
    C = q.shape[1]
    lg = ret_log_decay()
    i = jnp.arange(C, dtype=jnp.float32)
    diff = i[:, None] - i[None, :]
    decay = jnp.where(diff >= 0, jnp.exp(lg[:, None, None] * jnp.maximum(diff, 0.0)), 0.0)
    scores = jnp.einsum('bihd,bjhd->bhij', q, k) * decay[None]
    o_intra = jnp.einsum('bhij,bjhe->bihe', scores, v)
    q_dec = jnp.exp((i + 1.0)[:, None] * lg[None, :])
    o_cross = jnp.einsum('bihd,bhde->bihe', q, S) * q_dec[None, :, :, None]
    k_dec = jnp.exp((C - 1.0 - i)[:, None] * lg[None, :])
    S_new = (jnp.exp(C * lg)[None, :, None, None] * S
             + jnp.einsum('bjhd,bjhe->bhde', k * k_dec[None, :, :, None], v))
    return S_new, o_intra + o_cross

def retention_layer(x, pos, S0, chunk, norm_w, w_in, gn_w, w_out):
    B, T, _ = x.shape
    h = rmsnorm(x, norm_w) @ w_in
    qk_w = RET_HEADS * RET_DK
    q, k, v, g = jnp.split(h, [qk_w, 2 * qk_w, 2 * qk_w + RET_VW], axis=-1)
    q = rotary(q.reshape(B, T, RET_HEADS, RET_DK), pos)
    k = rotary(k.reshape(B, T, RET_HEADS, RET_DK), pos) * (RET_DK ** -0.5)
    v = v.reshape(B, T, RET_HEADS, RET_DV).astype(jnp.float32)
    n_chunks = T // chunk

    def to_chunks(a):
        return a.reshape(B, n_chunks, chunk, RET_HEADS, a.shape[-1]).swapaxes(0, 1)

    S_fin, o = lax.scan(lambda S, qkv: retention_chunk(S, *qkv), S0.astype(jnp.float32),
                        (to_chunks(q), to_chunks(k), to_chunks(v)))
    o = o.swapaxes(0, 1).reshape(B, T, RET_HEADS, RET_DV)
    o = rmsnorm(o, gn_w).reshape(B, T, RET_VW)
    y = (o * jax.nn.silu(g.astype(jnp.float32))).astype(x.dtype) @ w_out
    return x + y, S_fin

def shared_kv(x, kv_norm_w, w_kv, k_norm_w):
    B, T, _ = x.shape
    kv = rmsnorm(x, kv_norm_w) @ w_kv
    k, v = jnp.split(kv, 2, axis=-1)
    k = rmsnorm(k.reshape(B, T, MOBA_HEADS, MOBA_HD), k_norm_w)
    v = v.reshape(B, T, MOBA_HEADS, MOBA_HD)
    return k, v

def moba_query(x, norm_w, w_in, q_norm_w):
    B, T, _ = x.shape
    h = rmsnorm(x, norm_w) @ w_in
    q, g = jnp.split(h, 2, axis=-1)
    q = rmsnorm(q.reshape(B, T, MOBA_HEADS, MOBA_HD), q_norm_w) * (MOBA_HD ** -0.5)
    return q, g

def t5_bucket(dist):
    n = jnp.maximum(dist, 0)
    exact = REL_BUCKETS // 2
    big = exact + (jnp.log(jnp.maximum(n, 1).astype(jnp.float32) / exact)
                   / math.log(REL_MAX_DIST / exact) * (REL_BUCKETS - exact)).astype(jnp.int32)
    return jnp.where(n < exact, n, jnp.minimum(big, REL_BUCKETS - 1))

def moba_attend(q, q_pos, k_seq, v_seq, rel_bias):
    n_blk = k_seq.shape[0] // MOBA_BLOCK
    topk = min(MOBA_TOPK, n_blk)
    L = MOBA_BLOCK
    Q = q.shape[0]
    kb = k_seq.reshape(n_blk, L, MOBA_HEADS, MOBA_HD)
    vb = v_seq.reshape(n_blk, L, MOBA_HEADS, MOBA_HD)
    k_mean = jnp.mean(kb.astype(jnp.float32), axis=1)
    q_blk = q_pos // L
    gate = jnp.einsum('qhd,nhd->qhn', q.astype(jnp.float32), k_mean)
    fully_past = jnp.arange(n_blk)[None, None, :] < q_blk[:, None, None]
    gate = jnp.where(fully_past, gate, -jnp.inf)
    g_val, sel = lax.top_k(gate, topk)
    sel_ok = jnp.isfinite(g_val)
    h_idx = jnp.arange(MOBA_HEADS)[None, :, None]
    k_sel = kb.transpose(2, 0, 1, 3)[h_idx, sel]
    v_sel = vb.transpose(2, 0, 1, 3)[h_idx, sel]
    k_own = kb[q_blk]
    v_own = vb[q_blk]
    offs = jnp.arange(L, dtype=jnp.int32)
    pos_sel = sel[..., None] * L + offs
    pos_own = q_blk[:, None] * L + offs
    bias_h = rel_bias.T
    b_sel = bias_h[h_idx[..., None], t5_bucket(q_pos[:, None, None, None] - pos_sel)]
    b_own = bias_h[:, t5_bucket(q_pos[:, None] - pos_own)].transpose(1, 0, 2)
    s_sel = jnp.einsum('qhd,qhjld->qhjl', q, k_sel).astype(jnp.float32) + b_sel
    s_sel = jnp.where(sel_ok[..., None], s_sel, -jnp.inf)
    s_own = jnp.einsum('qhd,qlhd->qhl', q, k_own).astype(jnp.float32) + b_own
    s_own = jnp.where((pos_own <= q_pos[:, None])[:, None, :], s_own, -jnp.inf)
    logits = jnp.concatenate([s_sel.reshape(Q, MOBA_HEADS, topk * L), s_own], axis=-1)
    p = jax.nn.softmax(logits, axis=-1)
    p_sel = p[..., :topk * L].reshape(Q, MOBA_HEADS, topk, L).astype(v_sel.dtype)
    p_own = p[..., topk * L:].astype(v_own.dtype)
    return (jnp.einsum('qhjl,qhjld->qhd', p_sel, v_sel)
            + jnp.einsum('qhl,qlhd->qhd', p_own, v_own))

def moba_prompt(q, k, v, rel_bias):
    B, S = q.shape[:2]
    pad = (-S) % MOBA_BLOCK
    kp = jnp.pad(k, ((0, 0), (0, pad), (0, 0), (0, 0)))
    vp = jnp.pad(v, ((0, 0), (0, pad), (0, 0), (0, 0)))
    n_qb = S // MOBA_Q_BLOCK
    qb = q.reshape(B, n_qb, MOBA_Q_BLOCK, MOBA_HEADS, MOBA_HD)
    pos = jnp.arange(S, dtype=jnp.int32).reshape(n_qb, MOBA_Q_BLOCK)

    def per_seq(args):
        q_s, k_s, v_s = args
        return lax.map(lambda a: moba_attend(a[0], a[1], k_s, v_s, rel_bias), (q_s, pos))

    out = lax.map(per_seq, (qb, kp, vp))
    return out.reshape(B, S, MOBA_W)

def moba_sample(q, k_new, v_new, cache_k, cache_v, page_table, rel_bias):
    Bd, T = q.shape[:2]
    past = page_table.shape[1] * PAGE_SIZE
    pad = (-(past + T)) % MOBA_BLOCK
    q_pos = past + jnp.arange(T, dtype=jnp.int32)

    def per_seq(args):
        q_s, kn, vn, pages = args
        k_past = cache_k[pages].reshape(past, MOBA_HEADS, MOBA_HD)
        v_past = cache_v[pages].reshape(past, MOBA_HEADS, MOBA_HD)
        zpad = jnp.zeros((pad, MOBA_HEADS, MOBA_HD), k_past.dtype)
        k_s = jnp.concatenate([k_past, kn.astype(k_past.dtype), zpad], axis=0)
        v_s = jnp.concatenate([v_past, vn.astype(v_past.dtype), zpad.astype(v_past.dtype)], axis=0)
        return moba_attend(q_s, q_pos, k_s, v_s, rel_bias)

    out = lax.map(per_seq, (q, k_new, v_new, page_table))
    return out.reshape(Bd, T, MOBA_W)

def setup_inputs(seed: int = 0) -> dict:
    key = jax.random.key(seed)
    ks = jax.random.split(key, 20)
    n_pages = PAST_LEN // PAGE_SIZE
    n_used = DEC_BATCH * n_pages
    n_phys = n_used + n_used // 4

    def nrm(k, shape, scale):
        return jax.random.normal(k, shape, jnp.float32) * scale

    def gain(k, shape):
        return 1.0 + 0.02 * jax.random.normal(k, shape, jnp.float32)

    ret_in_w = 2 * RET_HEADS * RET_DK + 2 * RET_VW
    return {
        "x_prompt": nrm(ks[0], (BATCH, SEQ, D_MODEL), 1.0),
        "x_sample": nrm(ks[1], (DEC_BATCH, DEC_SEQ, D_MODEL), 1.0),
        "state_ret": nrm(ks[2], (N_RET_LAYERS, DEC_BATCH, RET_HEADS, RET_DK, RET_DV), RET_DK ** -0.5),
        "cache_k": nrm(ks[3], (n_phys, PAGE_SIZE, MOBA_HEADS, MOBA_HD), 1.0),
        "cache_v": nrm(ks[4], (n_phys, PAGE_SIZE, MOBA_HEADS, MOBA_HD), 1.0),
        "page_table": jax.random.permutation(ks[5], n_phys)[:n_used].reshape(DEC_BATCH, n_pages).astype(jnp.int32),
        "ret_norm_w": gain(ks[6], (N_RET_LAYERS, D_MODEL)),
        "ret_w_in": nrm(ks[7], (N_RET_LAYERS, D_MODEL, ret_in_w), D_MODEL ** -0.5),
        "ret_gn_w": gain(ks[8], (N_RET_LAYERS, RET_HEADS, RET_DV)),
        "ret_w_out": nrm(ks[9], (N_RET_LAYERS, RET_VW, D_MODEL), RET_VW ** -0.5),
        "kv_norm_w": gain(ks[10], (D_MODEL,)),
        "w_kv": nrm(ks[11], (D_MODEL, 2 * MOBA_W), D_MODEL ** -0.5),
        "k_norm_w": gain(ks[12], (MOBA_HD,)),
        "moba_norm_w": gain(ks[13], (N_MOBA_LAYERS, D_MODEL)),
        "moba_w_in": nrm(ks[14], (N_MOBA_LAYERS, D_MODEL, 2 * MOBA_W), D_MODEL ** -0.5),
        "q_norm_w": gain(ks[15], (N_MOBA_LAYERS, MOBA_HD)),
        "moba_w_out": nrm(ks[16], (N_MOBA_LAYERS, MOBA_W, D_MODEL), MOBA_W ** -0.5),
        "rel_bias": nrm(ks[17], (REL_BUCKETS, MOBA_HEADS), 0.5),
    }

def reference(x_prompt, x_sample, state_ret, cache_k, cache_v, page_table,
              ret_norm_w, ret_w_in, ret_gn_w, ret_w_out,
              kv_norm_w, w_kv, k_norm_w,
              moba_norm_w, moba_w_in, q_norm_w, moba_w_out, rel_bias):
    Bp, Tp, _ = x_prompt.shape
    Bs, Ts, _ = x_sample.shape
    pos_p = jnp.arange(Tp, dtype=jnp.int32)
    pos_s = PAST_LEN + jnp.arange(Ts, dtype=jnp.int32)
    hp, hs = x_prompt, x_sample
    st_p, st_s = [], []
    k_p = v_p = k_s = v_s = None
    for layer in range(DEPTH):
        if layer < N_RET_LAYERS:
            hp, sp = retention_layer(hp, pos_p, jnp.zeros((Bp, RET_HEADS, RET_DK, RET_DV), jnp.float32),
                                     RET_CHUNK, ret_norm_w[layer], ret_w_in[layer],
                                     ret_gn_w[layer], ret_w_out[layer])
            hs, ss = retention_layer(hs, pos_s, state_ret[layer], Ts, ret_norm_w[layer],
                                     ret_w_in[layer], ret_gn_w[layer], ret_w_out[layer])
            st_p.append(sp)
            st_s.append(ss)
            if layer == N_RET_LAYERS - 1:
                k_p, v_p = shared_kv(hp, kv_norm_w, w_kv, k_norm_w)
                k_s, v_s = shared_kv(hs, kv_norm_w, w_kv, k_norm_w)
        else:
            j = layer - N_RET_LAYERS
            qp, gp = moba_query(hp, moba_norm_w[j], moba_w_in[j], q_norm_w[j])
            op = moba_prompt(qp, k_p, v_p, rel_bias)
            hp = hp + ((op * jax.nn.silu(gp)).astype(hp.dtype) @ moba_w_out[j])
            qs, gs = moba_query(hs, moba_norm_w[j], moba_w_in[j], q_norm_w[j])
            os_ = moba_sample(qs, k_s, v_s, cache_k, cache_v, page_table, rel_bias)
            hs = hs + ((os_ * jax.nn.silu(gs)).astype(hs.dtype) @ moba_w_out[j])
    ret_state_prompt = jnp.stack(st_p, axis=0)
    ret_state_sample = jnp.stack(st_s, axis=0)
    return (hp, hs, ret_state_prompt, ret_state_sample, k_p, v_p, k_s, v_s)


_drawn_inputs = setup_inputs


def setup_inputs(seed=0):
    import zlib

    import numpy as np

    out = dict(_drawn_inputs(seed))
    spreads = {}
    factors = {'ret_gn_w': 5.472,
     'kv_norm_w': 2.907,
     'k_norm_w': 3.073,
     'moba_norm_w': 8.0,
     'q_norm_w': 8.0}
    for name, (base, spread) in spreads.items():
        noise = np.random.default_rng([zlib.crc32(name.encode()), seed]).standard_normal(out[name].shape)
        drawn = base * np.exp(spread * noise) if base else spread * noise
        out[name] = __import__('jax').numpy.asarray(drawn.astype(out[name].dtype))
    for name, factor in factors.items():
        out[name] = (out[name] * factor).astype(out[name].dtype)
    return out
```

```python
import math
from contextlib import ExitStack

import numpy as np

import concourse.bass as bass
from concourse import mybir

F32 = mybir.dt.float32
F32R = mybir.dt.float32r
I32 = mybir.dt.int32
ALU = mybir.AluOpType
ACT = mybir.ActivationFunctionType
AX = mybir.AxisListType

P = 128
D = 1024
KT = D // P
TP, TS = 256, 64
T = TP + TS
NSEQ, NEW = 8, 8
RH, DK, DV = 4, 256, 512
MH, HD = 8, 128
PAST, PAGE = 256, 128
NPG = PAST // PAGE
EPS = 1e-6
MASKED = -1e30
BUCKETS, MAX_DIST = 32, 128
CW = 2048
RAW = 3
NST = 5
NCP = 4
FAR = PAST + NEW - 1
LINE = 392
TOK = [(0, P), (P, P), (TP, TS)]

TILES = {"rq": 2, "rk": 2, "rv": 3, "rg": 2, "ro": 4, "mq": 2, "mk": 3, "mv": 3, "mg": 2, "mo": 3}

LOG_DECAY = [math.log1p(-(2.0 ** (-5 - h))) for h in range(RH)]

C_COS, C_SIN = 0, T
C_DT = 2 * T
C_DS = C_DT + RH * TP
C_QD = C_DS + RH * TS
C_KDP = C_QD + RH * TS
C_KDS = C_KDP + 2 * RH
C_QM = C_KDS + RH
C_N = C_QM + 4


def shape_constants():
    half = DK // 2
    inv = np.float32(10000.0) ** (-np.arange(half, dtype=np.float32) / half)
    pos = np.concatenate([np.arange(TP), PAST + np.tile(np.arange(NEW), NSEQ)]).astype(np.float32)
    ang = (pos[None, :] * inv[:, None].astype(np.float32)).astype(np.float32).astype(np.float64)
    lg = np.array(LOG_DECAY)
    scale = DK ** -0.5
    c = np.zeros((P, C_N))
    c[:, C_COS:C_COS + T] = np.cos(ang)
    c[:, C_SIN:C_SIN + T] = np.sin(ang)
    j, i = np.arange(P)[:, None, None], np.arange(TP)[None, None, :]
    c[:, C_DT:C_DS] = np.where(i >= j, np.exp(lg[None, :, None] * np.maximum(i - j, 0)) * scale, 0).reshape(P, -1)
    t = np.arange(TS)
    same = (t[:, None] // NEW == t[None, :] // NEW) & (t[None, :] >= t[:, None])
    gap = np.maximum(t[None, :] - t[:, None], 0)
    c[:TS, C_DS:C_QD] = (np.where(same, 1, 0)[:, None, :] * np.exp(lg[None, :, None] * gap[:, None, :]) * scale).reshape(TS, -1)
    c[:, C_QD:C_KDP] = np.exp((t % NEW + 1)[None, :] * lg[:, None]).reshape(1, -1)
    for tile in range(2):
        tok = tile * P + np.arange(P)
        c[:, C_KDP + tile * RH:C_KDP + (tile + 1) * RH] = np.exp((TP - 1 - tok)[:, None] * lg[None, :]) * scale
    c[:TS, C_KDS:C_KDS + RH] = np.exp((NEW - 1 - t % NEW)[:, None] * lg[None, :]) * scale
    c[:, C_QM:C_QM + 4] = (np.arange(P)[:, None] % 32) // NEW == np.arange(4)[None, :]
    eye = np.concatenate([np.eye(P), np.ones((P, P))], axis=1)
    dist = FAR - np.arange(FAR + 1)
    exact = BUCKETS // 2
    n = np.maximum(dist, 1).astype(np.float32)
    big = exact + (np.log(n / np.float32(exact)) / np.float32(math.log(MAX_DIST / exact))
                   * np.float32(BUCKETS - exact)).astype(np.int32)
    bucket = np.where(dist < exact, dist, np.minimum(big, BUCKETS - 1))
    hot = (bucket[None, :] == np.arange(BUCKETS)[:, None])
    return c.astype(np.float32), eye.astype(np.float32), hot.astype(np.float32)


def make_schedule():
    chunks, steps, use, used = [], [], {}, [0] * 8

    def fill(bank, *key):
        use[(*key, bank)] = used[bank]
        used[bank] += 1

    tiles = [0]

    def chunk(kind, a, b, gaps):
        c = len(chunks)
        chunks.append((kind, a, b))
        steps.append(("CHUNK", c))
        for i in range(TILES[kind]):
            j = tiles[0]
            tiles[0] += 1
            fill(j % 3, "TILE", c, i)
            steps.append(("TILE", c, i, j % 3))
            for s in gaps[i] if i < len(gaps) else []:
                add(*s)
        steps.append(("ENDCHUNK", c))

    banks = {"KT": (3, 4), "SC": (5,), "OP": (6, 7), "SF": (3, 4), "OSI": (5,), "U": (6, 7), "SS": (4,),
             "GNA": (), "BT": (6,), "NORM": (7,), "QS": (), "QSS": (7,), "QR": (), "KP": (3, 4), "KS": (), "ST": (5,),
             "KX": (6, 7), "SN": (6,), "SA": (5,), "SB": (6,), "PV": (), "OSM": (7,), "PG": (),
             "A": (3,), "B": (4,), "C": (6,), "XT": ()}

    def add(*s):
        for b in banks[s[0]]:
            fill(b, *s)
        steps.append(s)

    def states(h, b0, b1):
        return [[("U", h, b)] for b in range(b0, b1)]

    for kt in range(KT):
        fill(kt, "X", kt)
    steps.append(("X",))
    add("NORM", 0)
    for h in range(RH):
        if h == 3:
            u = states(2, 0, 4)
            chunk("ro", 0, 0, [u[0], [], u[1], []])
            chunk("ro", 0, 1, [u[2], [], u[3], []])
            u = states(2, 4, 8)
            u = [u[0], [], u[1], [], u[2], [], [], u[3], [], []]
        else:
            u = states(h - 1, 0, 8) + [[], []] if h else [[]] * 10
        chunk("rq", h, 0, u[0:2])
        chunk("rk", h, 0, u[2:4])
        chunk("rv", h, 0, u[4:7])
        chunk("rv", h, 1, u[7:9] + [u[9] + ([("GNA", h - 1)] if h else [])])
        chunk("rg", h, 0, [([("SS", h - 1)] if h else []) + [("KT", h)], [("SC", h)]])
        chunk("rg", h, 1, [[("OP", h)], [("SF", h), ("OSI", h)]])
    u = states(3, 0, 8)
    chunk("ro", 1, 0, u[0:4])
    chunk("ro", 1, 1, u[4:7] + [u[7] + [("GNA", 3)]])
    chunk("ro", 2, 0, [[("SS", 3)]])
    chunk("ro", 2, 1, [])
    chunk("ro", 3, 0, [[("BT",)]])
    chunk("ro", 3, 1, [])
    add("NORM", 1)
    fill(7, "QSS")
    for c in range(4):
        chunk("mq", c, 0, [[("QS", 2 * c)], [("QS", 2 * c + 1)]])
    steps.append(("QR",))
    kp = []
    for n in range(NSEQ * NPG):
        lag = [("KS", n - 1)] if n else []
        kp.append([("KP", n)] + lag)
        if n % 4 == 0:
            fill(5, "ST", n // 4)
    kp.append([("KS", 15)])
    for c in range(4):
        g = kp[3 * c:3 * c + 3]
        chunk("mk", c, 0, [g[0] + ([("KX", c - 1)] if c else []), g[1], g[2]])
    chunk("mv", 0, 0, [kp[12] + [("KX", 3)], kp[13], kp[14]])
    chunk("mv", 1, 0, [kp[15], kp[16] + [("SN",)], [("SA", 0)]])
    chunk("mv", 2, 0, [[("SA", 1), ("SB", 0)], [("SA", 2), ("SB", 1)], [("SA", 3), ("SB", 2)]])
    chunk("mv", 3, 0, [[("SB", 3), ("A", 0)], [("A", 1), ("B", 0)], [("A", 2), ("B", 1)]])
    fill(7, "OSM")
    for c in range(4):
        g = []
        for i in (2 * c, 2 * c + 1):
            s = ([("A", i + 3)] if i + 3 < MH else []) + ([("B", i + 2)] if i + 2 < MH else []) + [("C", i)]
            if i % 2 == 0:
                s.append(("PV", i // 2))
            if i == 7:
                s.insert(-1, ("PG",))
            g.append(s)
        chunk("mg", c, 0, g)
    for c in range(4):
        chunk("mo", c, 0, [])
    return chunks, steps, use


def build(nc, a):
    chunks, steps, use = make_schedule()
    nchunks = len(chunks)
    ctx = ExitStack()
    with ctx:
        def sb(name, shape, dt=F32, stack=ctx):
            return stack.enter_context(nc.sbuf_tensor(name, shape, dt))

        def sem(name):
            return ctx.enter_context(nc.semaphore(name))

        w_raw = sb("w_raw", [P, RAW, CW])
        w_hi = sb("w_hi", [P, 2, CW], F32R)
        w_lo = sb("w_lo", [P, 2, CW], F32R)
        xT = sb("xT", [P, KT, T])
        xn_hi = sb("xn_hi", [P, KT, T], F32R)
        xn_lo = sb("xn_lo", [P, KT, T], F32R)
        ym_hi = sb("ym_hi", [P, KT, T], F32R)
        ym_lo = sb("ym_lo", [P, KT, T], F32R)
        scr = sb("scr", [P, KT, T])
        eye = sb("eye", [P, 2 * P])
        ident, ones = eye[:, 0:P], eye[:, P:2 * P]
        wcols = sb("wcols", [P, 48])
        eps = sb("eps", [P, 2])
        rsb = sb("rsb", [P, T])
        W_RET, W_KV, W_MOBA, W_GN, W_Q = 0, 8, 16, 24, 40

        ret = ExitStack()
        def rb(name, shape, dt=F32):
            return sb(name, shape, dt, ret)
        st = rb("st", [P, NST, 2 * DV])
        cst = rb("cst", [P, C_N])
        wrow = rb("wrow", [41, P])
        raw_qk = rb("raw_qk", [P, 2, 2, T])
        rt = rb("rt", [P, 4, T])
        qT = rb("qT", [P, 2, T])
        kT = rb("kT", [P, 2, T])
        qd = rb("qd", [P, 2, 2, TS])
        vp = rb("vp", [P, 2, DV])
        vs = rb("vs", [TS, DV])
        vs_hi = rb("vs_hi", [TS, DV], F32R)
        vs_lo = rb("vs_lo", [TS, DV], F32R)
        vq = rb("vq", [P, 2, DV], F32R)
        kd = rb("kd", [P, 2, DK])
        ks = rb("ks", [TS, DK])
        ks_hi = rb("ks_hi", [TS, DK], F32R)
        ks_lo = rb("ks_lo", [TS, DK], F32R)
        kq = rb("kq", [P, 2, DK], F32R)
        km = rb("km", [P, 2, DK], F32R)
        gs = rb("gs", [P, 2, 4, T])
        sT = rb("sT", [P, TP + P])
        s2 = rb("s2", [TS, TS])
        fin = rb("fin", [P, 2, DV])
        ret.close()

        moba = ExitStack()
        def mb(name, shape, dt=F32):
            return sb(name, shape, dt, moba)
        cache = mb("cache", [P, NCP, D])
        mkT = mb("mkT", [P, MH, T])
        mqT = mb("mqT", [P, MH, T])
        mvp = mb("mvp", [P, 2, D])
        mvs = mb("mvs", [TS, D])
        rows = mb("rows", [P, 2, 3, 256])
        ktc = mb("ktc", [P, 2, MH, P])
        tb = mb("tb", [P, MH, TP])
        bs = mb("bs", [P, PAST])
        bn = mb("bn", [P, 4, TS])
        sst = mb("sst", [P, 4, 2 * P])
        sstn = mb("sstn", [TS, 4 * P])
        ps = mb("ps", [P, 2, T])
        pts, ptn = sst, sstn.ap().rearrange("j (s k) -> j s k", s=4)
        free = ktc.ap().rearrange("p s h k -> p s (h k)")[:, :, 0:2 * (TP + P)]
        pp = free[:, 0, :].rearrange("p (s k) -> p s k", s=2)
        pt = free[:, 1, :].rearrange("p (s k) -> p s k", s=2)
        sqs = mb("sqs", [P, NSEQ, MH, NEW])
        sqp = mb("sqp", [P, 2, TP])
        yf, yfs = sqp, sqs.ap().rearrange("p b h t -> p (b h t)").rearrange("p (h i) -> p h i", h=MH)
        junk = mb("junk", [P, P])
        knw = mb("knw", [P, HD])
        hot = mb("hot", [BUCKETS, FAR + 1])
        relb = mb("relb", [BUCKETS, MH])
        line = mb("line", [MH, LINE])
        pages = mb("pages", [1, NSEQ * NPG], I32)
        rsq = mb("rsq", [P, 20])
        kss = mb("kss", [P, 2, 2])
        nmx = mb("nmx", [P, 2, 2])
        den = mb("den", [P, 2, 2])
        nmxs = mb("nmxs", [P, 4])
        dens = mb("dens", [P, 4])
        moba.close()

        bank = [ctx.enter_context(nc.psum_tensor(f"bank{i}", [P, 512], F32)) for i in range(8)]
        scratch = nc.dram_tensor("bias_lines", (P, MH, LINE), F32, kind="Internal").ap()

        x_loaded, const_loaded, cst_loaded = sem("x_loaded"), sem("const_loaded"), sem("cst_loaded")
        w_loaded = [sem(f"w_loaded{i}") for i in range(RAW)]
        w_hi_done, w_lo_done = sem("w_hi_done"), sem("w_lo_done")
        bank_full = [sem(f"bank_full{i}") for i in range(8)]
        bank_read = [sem(f"bank_read{i}") for i in range(8)]
        eps_done = sem("eps_done")
        sq_done = sem("sq_done")
        unsplit_done = sem("unsplit_done")
        x_hi_done, x_lo_done = sem("x_hi_done"), sem("x_lo_done")
        rot_done = sem("rot_done")
        vs_hi_done, vs_lo_done = sem("vs_hi_done"), sem("vs_lo_done")
        ks_hi_done, ks_lo_done = sem("ks_hi_done"), sem("ks_lo_done")
        vq_loaded, kq_loaded, km_done = sem("vq_loaded"), sem("kq_loaded"), sem("km_done")
        osi_done = sem("osi_done")
        y_done, y_hi_done, y_lo_done = sem("y_done"), sem("y_hi_done"), sem("y_lo_done")
        fin_stored = sem("fin_stored")
        st_loaded = [sem(f"st_loaded{i}") for i in range(NST)]
        st_stored = [sem(f"st_stored{i}") for i in range(NST)]
        act_steps, dve_steps, pool_steps = sem("act_steps"), sem("dve_steps"), sem("pool_steps")
        moba_loaded, pages_loaded = sem("moba_loaded"), sem("pages_loaded")
        line_stored, bias_loaded, bn_masked = sem("line_stored"), sem("bias_loaded"), sem("bn_masked")
        qs_done = sem("qs_done")
        cache_loaded = [sem(f"cache_loaded{i}") for i in range(NCP)]
        ks_done = sem("ks_done")
        pv_done = sem("pv_done")
        kss_done = sem("kss_done")
        rows_stored = [sem("rows_stored0"), sem("rows_stored1")]
        sa_max, sa_exp, sa_done = sem("sa_max"), sem("sa_exp"), sem("sa_done")
        a_max, a_exp, a_done = sem("a_max"), sem("a_exp"), sem("a_done")
        stored = sem("stored")

        class Steps:
            def __init__(self, eng, s):
                self.eng, self.s, self.n = eng, s, 0

            def __call__(self, ins):
                ins.then_inc(self.s, 1)
                self.n += 1

            def wait(self):
                self.eng.wait_ge(self.s, self.n)

        def await_free(pe, b, *key):
            if use[(*key, b)]:
                pe.wait_ge(bank_read[b], use[(*key, b)])

        def await_full(eng, b, *key):
            eng.wait_ge(bank_full[b], use[(*key, b)] + 1)

        def await_read(eng, b, *key):
            eng.wait_ge(bank_read[b], use[(*key, b)] + 1)

        def await_ks(eng, n):
            if n < 0:
                return
            if n % 4 == 3:
                await_full(eng, 5, "ST", n // 4)
            else:
                eng.wait_ge(ks_done, n + 1 - (n + 1) // 4)

        def tile_use(kind, i):
            c = [k for k, x in enumerate(chunks) if x[0] == kind][i // TILES[kind]]
            return next((s[3], *s[:3]) for s in steps if s[:3] == ("TILE", c, i % TILES[kind]))

        def last_tile(c):
            return next((s[3], *s[:3]) for s in steps if s[:3] == ("TILE", c, TILES[chunks[c][0]] - 1))

        def chunk_source(c):
            kind, h, i = chunks[c]
            if kind[0] == "r" and kind != "ro":
                col = {"rq": h * DK, "rk": RH * DK + h * DK, "rv": 2 * RH * DK + h * DV + i * 256,
                       "rg": 2 * RH * DK + RH * DV + h * DV + i * 256}[kind]
                return a["ret_w_in"][0].rearrange("(k p) n -> p k n", p=P)[:, :, col:col + 256]
            if kind == "ro":
                return a["ret_w_out"][0].rearrange("(k p) n -> p k n", p=P)[:, 4 * h:4 * h + 4, 512 * i:512 * i + 512]
            src, off = {"mq": (a["moba_w_in"][0], 0), "mg": (a["moba_w_in"][0], D), "mk": (a["w_kv"], 0),
                        "mv": (a["w_kv"], D), "mo": (a["moba_w_out"][0], 0)}[kind]
            return src.rearrange("(k p) n -> p k n", p=P)[:, :, off + 256 * h:off + 256 * h + 256]

        def chunk_view(buf, c, s):
            n = 512 if chunks[c][0] == "ro" else 256
            return buf[:, s, :].rearrange("p (k n) -> p k n", n=n)

        st_dram = a["state_ret"][0].rearrange("b h (k p) e -> b h p k e", p=P)
        st_out = a["ret_state_sample"][0].rearrange("b h (k p) e -> b h p k e", p=P)
        x_rows = [a["x_prompt"][0, 0:P], a["x_prompt"][0, P:TP], a["x_sample"].rearrange("b t d -> (b t) d")]

        def out_rows(name):
            p, s = a[f"{name}_prompt"], a[f"{name}_sample"]
            if name != "y":
                p, s = p.rearrange("b t h d -> b t (h d)"), s.rearrange("b t h d -> b t (h d)")
            return [p[0, 0:P], p[0, P:TP], s.rearrange("b t d -> (b t) d")]

        k_out, v_out, y_out = out_rows("k"), out_rows("v"), out_rows("y")
        block = ctx.enter_context(nc.Block())

        @block.sync
        def _(sp):
            n_stored = [0]

            def store(dst, src):
                sp.dma_start(dst, src).then_inc(stored, 16)
                n_stored[0] += 16

            def load_chunk(c):
                if c >= nchunks:
                    return
                if c >= RAW:
                    sp.wait_ge(w_lo_done, c - RAW + 1)
                sp.dma_start(chunk_view(w_raw, c, c % RAW), chunk_source(c)).then_inc(w_loaded[c % RAW], 16)

            def load_state(s):
                if s >= RH * NSEQ:
                    return
                if s >= NST:
                    sp.wait_ge(st_stored[s % NST], 16 * (s // NST))
                elif s < 3:
                    await_full(sp, KT - 1, "X", KT - 1)
                sp.dma_start(st[:, s % NST, :].rearrange("p (k e) -> p k e", k=2),
                             st_dram[s % NSEQ, s // NSEQ]).then_inc(st_loaded[s % NST], 16)

            def store_state(s):
                await_read(sp, 6, "U", s // NSEQ, s % NSEQ)
                await_read(sp, 7, "U", s // NSEQ, s % NSEQ)
                sp.dma_start(st_out[s % NSEQ, s // NSEQ],
                             st[:, s % NST, :].rearrange("p (k e) -> p k e", k=2)).then_inc(st_stored[s % NST], 16)

            def load_page(n):
                m, vals = n % 16, n >= 16
                if n >= 16 + NCP:
                    sp.wait_ge(pv_done, (n - 16) // NCP)
                elif n >= NCP:
                    await_full(sp, 4, "KP", n - NCP)
                else:
                    await_read(sp, 7, "NORM", 1)
                page = sp.value_load(pages[0:1, m:m + 1], min_val=0, max_val=a["cache_k"].shape[0] - 1)
                src = a["cache_v"] if vals else a["cache_k"]
                sp.dma_start(cache[:, n % NCP, :], src[bass.ds(page, 1)].rearrange("o p h d -> p (o h d)"))\
                    .then_inc(cache_loaded[n % NCP], 16)

            sp.dma_start(eye[:, :], a["c_eye"]).then_inc(const_loaded, 16)
            for t, (c0, m) in enumerate(TOK):
                sp.dma_start(st[0:m, t, :], x_rows[t]).then_inc(x_loaded, 16)
            for r0, name, n in ((W_RET, "ret_norm_w", 8), (W_KV, "kv_norm_w", 8), (W_MOBA, "moba_norm_w", 8),
                                (W_GN, "ret_gn_w", 16), (W_Q, "q_norm_w", 1)):
                v = a[name]
                v = {1: lambda: v, 2: lambda: v.rearrange("a n -> (a n)"),
                     3: lambda: v.rearrange("a h n -> (a h n)")}[len(v.shape)]()
                sp.dma_start(wrow[r0:r0 + n, :], v.rearrange("(r p) -> r p", p=P)).then_inc(const_loaded, 16)
            load_chunk(0)
            sp.dma_start(cst[:, :], a["c_ret"]).then_inc(cst_loaded, 16)
            load_chunk(1)

            for step in steps:
                kind = step[0]
                if kind == "CHUNK":
                    c = step[1]
                    load_chunk(c + 2)
                    if c == 2:
                        for s in range(3):
                            load_state(s)
                elif kind == "KT":
                    h = step[1]
                    sp.wait_ge(vs_lo_done, 2 * (h + 1))
                    if h:
                        await_full(sp, 7, "U", h - 1, NSEQ - 1)
                    for g in range(2):
                        for term, src in enumerate((vs_hi, vs_lo, vs_hi, vs_lo)):
                            sp.dma_start(vq[32 * term:32 * term + 32, g, :].bitcast(F32), src[32 * g:32 * g + 32, :].bitcast(F32))\
                                .then_inc(vq_loaded, 16)
                elif kind == "SC":
                    h = step[1]
                    sp.wait_ge(ks_lo_done, h + 1)
                    if h:
                        sp.wait_ge(km_done, NSEQ * h)
                    for g in range(2):
                        for term, src in enumerate((ks_hi, ks_hi, ks_lo, ks_lo)):
                            sp.dma_start(kq[32 * term:32 * term + 32, g, :].bitcast(F32), src[32 * g:32 * g + 32, :].bitcast(F32))\
                                .then_inc(kq_loaded, 16)
                elif kind == "U":
                    s = step[1] * NSEQ + step[2]
                    if s:
                        store_state(s - 1)
                    load_state(s + 3)
                    if step[2] == 1:
                        await_read(sp, 3, "SF", step[1])
                        await_read(sp, 4, "SF", step[1])
                        sp.dma_start(a["ret_state_prompt"][0, 0, step[1]].rearrange("(k p) e -> p k e", p=P),
                                     fin[:, :, :]).then_inc(fin_stored, 16)
                elif kind == "BT":
                    store_state(RH * NSEQ - 1)
                    for s in range(RH * NSEQ - NST, RH * NSEQ):
                        sp.wait_ge(st_stored[s % NST], 16 * (s // NST + 1))
                    sp.wait_ge(fin_stored, 16 * RH)
                    sp.wait_ge(y_lo_done, RH)
                    sp.dma_start(hot[:, :], a["c_hot"]).then_inc(moba_loaded, 16)
                    sp.dma_start(relb[:, :], a["rel_bias"]).then_inc(moba_loaded, 16)
                    sp.dma_start(knw[:, :], bass.AP(a["k_norm_w"].tensor, 0, [[0, P], [1, HD]])).then_inc(moba_loaded, 16)
                    sp.dma_start(pages[:, :], a["page_table"].rearrange("b n -> (b n)").rearrange("(o n) -> o n", o=1))\
                        .then_inc(pages_loaded, 16)
                elif kind == "NORM" and step[1] == 1:
                    await_read(sp, 6, "BT")
                    sp.dma_start(scratch.rearrange("r h u -> h r u"),
                                 line[:, :].rearrange("h (o u) -> h o u", o=1).broadcast_to((MH, P, LINE)))\
                        .then_inc(line_stored, 16)
                    sp.wait_ge(line_stored, 16)
                    lines, skew = scratch.tensor, MH * LINE - 1
                    sp.dma_start(tb[:, :, :], bass.AP(lines, FAR - P, [[skew, P], [LINE, MH], [1, TP]])).then_inc(bias_loaded, 16)
                    for b2 in range(2):
                        sp.dma_start(bs[TS * b2:TS * b2 + TS, :],
                                     bass.AP(lines, FAR - PAST, [[LINE, MH], [skew, NEW], [1, PAST]])).then_inc(bias_loaded, 16)
                    sp.wait_ge(bn_masked, 1)
                    for pair in range(4):
                        for b2 in range(2):
                            c0 = (2 * pair + b2) * NEW
                            sp.dma_start(bn[TS * b2:TS * b2 + TS, pair, c0:c0 + NEW],
                                         bass.AP(lines, FAR, [[LINE, MH], [skew, NEW], [1, NEW]])).then_inc(bias_loaded, 16)
                    sp.wait_ge(pages_loaded, 16)
                    for n in range(NCP):
                        load_page(n)
                elif kind == "KP":
                    n = step[1]
                    if 1 <= n <= 12:
                        load_page(n + 3)
                elif kind == "KX":
                    c = step[1]
                    for t in range(3):
                        await_read(sp, *tile_use("mk", 3 * c + t))
                    for t, (c0, m) in enumerate(TOK):
                        sp.dma_start(k_out[t][:, 256 * c:256 * c + 256], rows[0:m, c % 2, t, :])\
                            .then_inc(rows_stored[c % 2], 16)
                elif kind == "SN":
                    for n in range(16, 20):
                        load_page(n)
                elif kind == "PV":
                    for n in range(20 + 4 * step[1], min(24 + 4 * step[1], 32)):
                        load_page(n)
                elif kind == "A" and step[1] == 3:
                    for t in range(3):
                        await_read(sp, *tile_use("mv", 9 + t))
                    for t, (c0, m) in enumerate(TOK):
                        store(v_out[t], mvp[:, t, :] if t < 2 else mvs[:, :])
                elif kind == "ENDCHUNK" and chunks[step[1]][0] == "mo":
                    c = chunks[step[1]][1]
                    for t, (c0, m) in enumerate(TOK):
                        await_read(sp, *tile_use("mo", 3 * c + t))
                        sp.dma_start(y_out[t][:, 256 * c:256 * c + 256], rows[0:m, c % 2, t, :])\
                            .then_inc(rows_stored[c % 2], 16)
            for s in range(RH * NSEQ - NST, RH * NSEQ):
                sp.wait_ge(st_stored[s % NST], 16 * (s // NST + 1))
            sp.wait_ge(fin_stored, 16 * RH)
            for r in rows_stored:
                sp.wait_ge(r, 4 * 48)
            sp.wait_ge(stored, n_stored[0])

        @block.tensor
        def _(pe):
            def close(mm, b):
                mm.then_inc(bank_full[b], 1)

            def project(step):
                _, c, i, b = step
                kind, h, part = chunks[c]
                if i == 0:
                    pe.wait_ge(w_lo_done, c + 1)
                await_free(pe, b, "TILE", c, i)
                hi, lo = chunk_view(w_hi, c, c % 2), chunk_view(w_lo, c, c % 2)
                x_hi, x_lo, k0, nk = xn_hi, xn_lo, 0, KT
                if kind in ("mq", "mg"):
                    x_hi, x_lo = ym_hi, ym_lo
                if kind == "ro":
                    x_hi, x_lo, k0, nk = ym_hi, ym_lo, 4 * (h % 2), 4
                    if i == 0 and part == 0:
                        pe.wait_ge(y_lo_done, h + 1)
                first = {"rq": 8, "mq": 16, "mk": 24}.get(kind) if h == 0 and i == 0 and part == 0 else None
                if kind == "mo" and h == 0 and i == 0:
                    pe.wait_ge(x_lo_done, 24 + MH + 1)
                for k in range(nk):
                    if first:
                        pe.wait_ge(x_lo_done, first - 8 + k + 1)
                    for n, (w, x) in enumerate(((hi, x_hi), (hi, x_lo), (lo, x_hi))):
                        flags = {"start": k == 0 and n == 0, "stop": k == nk - 1 and n == 2 and kind != "mo"}
                        if kind in ("rv", "mk", "mv", "mo"):
                            c0, m = TOK[i]
                            mm = pe.matmul(bank[b][0:m, 0:256], x[:, k, c0:c0 + m], w[:, k, :], **flags)
                        else:
                            mm = pe.matmul(bank[b][:, 0:T], w[:, k, P * i:P * i + P], x[:, k0 + k, :], **flags)
                if kind == "mo":
                    c0, m = TOK[i]
                    for k in range(2):
                        mm = pe.matmul(bank[b][0:m, P * k:P * k + P], xT[:, 2 * h + k, c0:c0 + m], ident,
                                       start=False, stop=k == 1)
                close(mm, b)

            for step in steps:
                kind = step[0]
                if kind == "X":
                    pe.wait_ge(x_loaded, 48)
                    pe.wait_ge(const_loaded, 16 * 6)
                    for kt in range(KT):
                        for t, (c0, m) in enumerate(TOK):
                            mm = pe.transpose(bank[kt][:, c0:c0 + m], st[0:m, t, P * kt:P * kt + P], ident[0:m, 0:m])
                        if kt == 0:
                            mm = pe.transpose(bank[0][:, 384:425], wrow[:, :], ident[0:41, 0:41])
                        close(mm, kt)
                elif kind == "NORM":
                    await_free(pe, 7, "NORM", step[1])
                    for kt in range(KT):
                        pe.wait_ge(sq_done, 12 * step[1] + kt + 1)
                        mm = pe.matmul(bank[7][:, 0:T], ones, scr[:, kt, :], start=kt == 0, stop=kt == KT - 1)
                    close(mm, 7)
                elif kind == "TILE":
                    project(step)
                elif kind == "ENDCHUNK":
                    pass
                elif kind == "KT":
                    h = step[1]
                    pe.wait_ge(rot_done, 2 * (h + 1))
                    await_free(pe, 3, *step)
                    for t in range(2):
                        for d in range(2):
                            mm = pe.transpose(bank[3][:, DK * t + P * d:DK * t + P * d + P], kT[:, d, P * t:P * t + P], ident)
                    close(mm, 3)
                    await_free(pe, 4, *step)
                    for d in range(2):
                        mm = pe.transpose(bank[4][0:TS, P * d:P * d + P], kT[:, d, TP:T], ident)
                    close(mm, 4)
                elif kind == "SC":
                    await_free(pe, 5, *step)
                    for col, n, j, m, i0 in ((0, TP, 0, P, 0), (TP, P, P, P, P), (TP + P, TS, TP, TS, TP)):
                        for d in range(2):
                            mm = pe.matmul(bank[5][0:m, col:col + n], kT[:, d, j:j + m], qT[:, d, i0:i0 + n],
                                           start=d == 0, stop=d == 1)
                    close(mm, 5)
                elif kind == "OP":
                    h = step[1]
                    await_read(pe, 5, "SC", h)
                    for i in range(6 * h, 6 * h + 6):
                        await_read(pe, *tile_use("rv", i))
                    for e in range(4):
                        b = 6 + e // 2
                        if e % 2 == 0:
                            await_free(pe, b, *step)
                        o = bank[b][:, TP * (e % 2):TP * (e % 2) + TP]
                        pe.matmul(o, vp[:, 0, P * e:P * e + P], sT[:, 0:TP], start=True, stop=False)
                        mm = pe.matmul(o[:, P:TP], vp[:, 1, P * e:P * e + P], sT[:, TP:TP + P], start=False, stop=True)
                        if e % 2:
                            close(mm, b)
                elif kind == "SF":
                    await_read(pe, 3, "KT", step[1])
                    for d in range(2):
                        await_free(pe, 3 + d, *step)
                        for t in range(2):
                            mm = pe.matmul(bank[3 + d][:, :], kd[:, t, P * d:P * d + P], vp[:, t, :],
                                           start=t == 0, stop=t == 1)
                        close(mm, 3 + d)
                elif kind == "OSI":
                    await_free(pe, 5, *step)
                    for e in range(4):
                        mm = pe.matmul(bank[5][:, TS * e:TS * e + TS], vs[:, P * e:P * e + P], s2[:, :],
                                       start=e == 0, stop=False, skip_group_check=True)
                    mm.then_inc(osi_done, 1)
                elif kind == "U":
                    h, b = step[1:]
                    s = NSEQ * h + b
                    pe.wait_ge(st_loaded[s % NST], 16 * (s // NST + 1))
                    for e in range(4):
                        for d in range(2):
                            mm = pe.matmul(bank[5][:, TS * e + NEW * b:TS * e + NEW * b + NEW],
                                           st[:, s % NST, DV * d + P * e:DV * d + P * e + P],
                                           qd[:, h % 2, d, NEW * b:NEW * b + NEW],
                                           start=False, stop=b == NSEQ - 1 and d == 1, skip_group_check=True)
                    if b == NSEQ - 1:
                        close(mm, 5)
                    if b == 0:
                        pe.wait_ge(vq_loaded, 128 * (h + 1))
                    pe.wait_ge(km_done, s + 1)
                    for d in range(2):
                        await_free(pe, 6 + d, *step)
                        close(pe.matmul(bank[6 + d][:, :], km[:, s % 2, P * d:P * d + P], vq[:, b // 4, :],
                                        start=True, stop=True), 6 + d)
                elif kind == "SS":
                    pe.wait_ge(sq_done, 8 + step[1] + 1)
                    await_free(pe, 4, *step)
                    for e in range(4):
                        mm = pe.matmul(bank[4][:, 0:T], ones, scr[:, 4 + e, :], start=e == 0, stop=e == 3)
                    close(mm, 4)
                elif kind == "BT":
                    pe.wait_ge(moba_loaded, 48)
                    await_free(pe, 6, *step)
                    close(pe.matmul(bank[6][0:MH, 0:FAR + 1], relb[:, :], hot[:, :], start=True, stop=True), 6)
                elif kind == "QS":
                    h = step[1]
                    await_read(pe, *tile_use("mq", h))
                    if h == 0:
                        await_free(pe, 7, "QSS")
                    for t in range(2):
                        mm = pe.matmul(bank[7][:, 2 * h + t:2 * h + t + 1], sqp[:, h % 2, P * t:P * t + P], ones[:, 0:1],
                                       start=True, stop=True)
                    if h < MH - 1:
                        mm.then_inc(qs_done, 1)
                    else:
                        for pair in range(4):
                            mm = pe.matmul(bank[7][:, 16 + pair:17 + pair],
                                           sqs[:, 2 * pair:2 * pair + 2].rearrange("p b h t -> p (b h t)"), ones[:, 0:1],
                                           start=True, stop=True)
                        close(mm, 7)
                elif kind == "KP":
                    n = step[1]
                    pe.wait_ge(cache_loaded[n % NCP], 16 * (n // NCP + 1))
                    for h in range(MH):
                        b = 3 + h // 4
                        if h % 4 == 0:
                            await_free(pe, b, *step)
                        mm = pe.transpose(bank[b][:, P * (h % 4):P * (h % 4) + P], cache[:, n % NCP, P * h:P * h + P], ident)
                        if h % 4 == 3:
                            close(mm, b)
                elif kind == "KS":
                    n = step[1]
                    b, pg = n // 2, n % 2
                    await_read(pe, 3, "KP", n)
                    await_read(pe, 4, "KP", n)
                    if n % 4 == 0:
                        await_free(pe, 5, "ST", n // 4)
                    for h in range(MH):
                        col = P * pg + TS * (b % 2) + NEW * h
                        mm = pe.matmul(bank[5][:, col:col + NEW], ktc[:, n % 2, h, :], mqT[:, h, TP + NEW * b:TP + NEW * b + NEW],
                                       start=True, stop=True)
                    if n % 4 == 3:
                        close(mm, 5)
                    else:
                        mm.then_inc(ks_done, 1)
                elif kind == "KX":
                    c = step[1]
                    for t in range(3):
                        await_read(pe, *tile_use("mk", 3 * c + t))
                    for i in range(2):
                        await_free(pe, 6 + i, *step)
                        for t, (c0, m) in enumerate(TOK):
                            mm = pe.transpose(bank[6 + i][:, c0:c0 + m], rows[0:m, c % 2, t, P * i:P * i + P], ident[0:m, 0:m])
                        close(mm, 6 + i)
                elif kind == "SN":
                    await_free(pe, 6, *step)
                    await_read(pe, 6, "KX", 3)
                    await_read(pe, 7, "KX", 3)
                    o = bank[6][0:TS, :].rearrange("p (b h t) -> p b h t", b=NSEQ, h=MH)
                    for h in range(MH):
                        mm = pe.matmul(o[:, :, h, :], mkT[:, h, TP:T], mqT[:, h, TP:T], start=True, stop=True)
                    close(mm, 6)
                elif kind == "SA":
                    pair = step[1]
                    if pair == 0:
                        await_read(pe, 5, "ST", 3)
                        await_read(pe, 6, "SN")
                    await_free(pe, 5, *step)
                    for pg in range(2):
                        pe.transpose(bank[5][:, P * pg:P * pg + P], sst[:, pair, P * pg:P * pg + P], ident)
                    close(pe.transpose(bank[5][:, PAST:PAST + TS], sstn[:, P * pair:P * pair + P], ident[0:TS, 0:TS]), 5)
                elif kind == "SB":
                    pair = step[1]
                    pe.wait_ge(sa_done, pair + 1)
                    await_free(pe, 6, *step)
                    for pg in range(2):
                        pe.transpose(bank[6][:, P * pg:P * pg + P], ps[:, pair % 2, P * pg:P * pg + P], ident)
                    close(pe.transpose(bank[6][0:TS, PAST:PAST + P], ps[:, pair % 2, PAST:T], ident), 6)
                elif kind == "PV":
                    pair = step[1]
                    await_read(pe, 6, "SB", pair)
                    if pair == 0:
                        await_free(pe, 7, "OSM")
                        await_read(pe, *tile_use("mv", 11))
                    for b2 in range(2):
                        b = 2 * pair + b2
                        for pg in range(2):
                            n = 16 + 2 * b + pg
                            pe.wait_ge(cache_loaded[n % NCP], 16 * (n // NCP + 1))
                        for h in range(MH):
                            o = bank[7][:, TS * h + NEW * b:TS * h + NEW * b + NEW]
                            r = TS * b2 + NEW * h
                            for pg in range(2):
                                pe.matmul(o, cache[:, (16 + 2 * b + pg) % NCP, P * h:P * h + P],
                                          pts[:, pair, P * pg + r:P * pg + r + NEW], start=pg == 0, stop=False)
                            mm = pe.matmul(o, mvs[:, P * h:P * h + P], ptn[:, pair, r:r + NEW], start=False, stop=True)
                    if pair == 3:
                        close(mm, 7)
                    else:
                        mm.then_inc(pv_done, 1)
                elif kind == "A":
                    h = step[1]
                    if h == 0:
                        await_read(pe, 6, "KX", 3)
                        await_read(pe, 7, "KX", 3)
                    await_free(pe, 3, *step)
                    pe.matmul(bank[3][:, 0:TP], mqT[:, h, P:TP], mkT[:, h, 0:TP], start=True, stop=True)
                    close(pe.matmul(bank[3][:, TP:TP + P], mqT[:, h, 0:P], mkT[:, h, 0:P], start=True, stop=True), 3)
                elif kind == "B":
                    h = step[1]
                    pe.wait_ge(a_done, h + 1)
                    await_free(pe, 4, *step)
                    for i, col in enumerate((TP, 0, P)):
                        mm = pe.transpose(bank[4][:, P * i:P * i + P], pp[:, h % 2, col:col + P], ident)
                    close(mm, 4)
                elif kind == "C":
                    h = step[1]
                    await_read(pe, 4, "B", h)
                    await_free(pe, 6, *step)
                    pe.matmul(bank[6][:, 0:TP], mvp[:, 0, P * h:P * h + P], pt[:, h % 2, 0:TP], start=True, stop=False)
                    close(pe.matmul(bank[6][:, P:TP], mvp[:, 1, P * h:P * h + P], pt[:, h % 2, TP:TP + P],
                                    start=False, stop=True), 6)

        @block.scalar
        def _(act):
            done = Steps(act, act_steps)

            def split_hi(c):
                if c >= nchunks:
                    return
                act.wait_ge(w_loaded[c % RAW], 16 * (c // RAW + 1))
                if c >= 2:
                    await_full(act, *last_tile(c - 2))
                act.activation(w_hi[:, c % 2, :], w_raw[:, c % RAW, :], ACT.Copy).then_inc(w_hi_done, 1)

            act.wait_ge(eps_done, 1)
            nk = 0
            nx = 0
            for step in steps:
                kind = step[0]
                if kind == "CHUNK":
                    split_hi(step[1] + 1)
                elif kind == "NORM":
                    w = step[1]
                    for kt in range(KT):
                        if w:
                            await_read(act, *tile_use("ro", 24 + kt))
                            if kt == 0:
                                act.wait_ge(y_lo_done, RH)
                        else:
                            await_read(act, kt, "X", kt)
                        act.activation(scr[:, kt, :], xT[:, kt, :], ACT.Square).then_inc(sq_done, 1)
                    if w == 0:
                        split_hi(0)
                    await_full(act, 7, *step)
                    act.activation(rsb[:, :], bank[7][:, 0:T], ACT.Sqrt, bias=eps[:, 0:1], scale=1.0 / D)\
                        .then_inc(bank_read[7], 1)
                    for n in range(2 if w else 1):
                        dst = ym_hi if w and n == 0 else xn_hi
                        if w and n == 1:
                            await_full(act, *tile_use("rg", 15))
                        for kt in range(KT):
                            nx += 1
                            act.wait_ge(unsplit_done, nx)
                            act.activation(dst[:, kt, :], scr[:, kt, :], ACT.Copy).then_inc(x_hi_done, 1)
                elif kind == "TILE":
                    c, i, b = step[1:]
                    what, h, part = chunks[c]
                    if what == "ro":
                        continue
                    if what == "mo" and (3 * h + i) % 2:
                        continue
                    await_full(act, b, *step[:3])
                    if what in ("rq", "rk"):
                        qk = int(what == "rk")
                        if h:
                            act.wait_ge(rot_done, 2 * h - 1 + qk)
                        act.activation(raw_qk[:, qk, i, :], bank[b][:, 0:T], ACT.Copy).then_inc(bank_read[b], 1)
                    elif what == "rv" and i < 2:
                        if h:
                            await_full(act, 4, "SF", h - 1)
                        act.activation(vp[:, i, 256 * part:256 * part + 256], bank[b][:, 0:256], ACT.Copy)\
                            .then_inc(bank_read[b], 1)
                    elif what == "rv":
                        cols = slice(256 * part, 256 * part + 256)
                        if h:
                            act.wait_ge(osi_done, h)
                            act.wait_ge(vs_lo_done, 2 * h)
                            act.wait_ge(vq_loaded, 128 * h)
                        act.activation(vs[:, cols], bank[b][0:TS, 0:256], ACT.Copy).then_inc(bank_read[b], 1)
                        await_read(act, b, *step[:3])
                        act.activation(vs_hi[:, cols], vs[:, cols], ACT.Copy).then_inc(vs_hi_done, 1)
                    elif what == "rg":
                        if h >= 2:
                            act.wait_ge(y_done, h - 1)
                        act.activation(gs[:, h % 2, 2 * part + i, :], bank[b][:, 0:T], ACT.Silu).then_inc(bank_read[b], 1)
                    elif what == "mq":
                        head = 2 * h + i
                        if head >= 2:
                            act.wait_ge(qs_done, head - 1)
                        act.activation(sqp[:, head % 2, :], bank[b][:, 0:TP], ACT.Square)
                        act.activation(sqs[:, :, head, :], bank[b][:, TP:T].rearrange("p (b t) -> p b t", t=NEW), ACT.Square)
                        act.activation(mqT[:, head, :], bank[b][:, 0:T], ACT.Copy, scale=wcols[:, W_Q:W_Q + 1])\
                            .then_inc(bank_read[b], 1)
                    elif what == "mk":
                        m = TOK[i][1]
                        if nk >= 2:
                            await_read(act, *tile_use("mk", nk - 2))
                        for d in range(2):
                            if nk or d:
                                done.wait()
                            done(act.activation(junk[0:m, :], bank[b][0:m, P * d:P * d + P], ACT.Square,
                                                accum_out=kss[0:m, nk % 2, d:d + 1]))
                        done.wait()
                        act.activation(kss[0:m, nk % 2, :], kss[0:m, nk % 2, :], ACT.Sqrt, bias=eps[0:m, 0:1], scale=1.0 / HD)\
                            .then_inc(kss_done, 1)
                        nk += 1
                    elif what == "mv":
                        dst = mvp[:, i, 256 * h:256 * h + 256] if i < 2 else mvs[:, 256 * h:256 * h + 256]
                        act.activation(dst, bank[b][0:TOK[i][1], 0:256], ACT.Copy).then_inc(bank_read[b], 1)
                    elif what == "mg":
                        if h == 0 and i == 0:
                            act.wait_ge(x_lo_done, 24)
                        act.activation(scr[:, 2 * h + i, :], bank[b][:, 0:T], ACT.Silu).then_inc(bank_read[b], 1)
                    elif what == "mo":
                        act.wait_ge(rows_stored[h % 2], 48 * (2 + h // 2))
                        act.activation(rows[0:TOK[i][1], h % 2, i, :], bank[b][0:TOK[i][1], 0:256], ACT.Copy)\
                            .then_inc(bank_read[b], 1)
                elif kind == "KT":
                    h = step[1]
                    await_full(act, 3, *step)
                    if h:
                        await_full(act, 4, "SF", h - 1)
                    for t in range(2):
                        ins = act.activation(kd[:, t, :], bank[3][:, DK * t:DK * t + DK], ACT.Copy,
                                             scale=cst[:, C_KDP + RH * t + h:C_KDP + RH * t + h + 1])
                    ins.then_inc(bank_read[3], 1)
                    await_full(act, 4, *step)
                    if h:
                        act.wait_ge(ks_lo_done, h)
                        act.wait_ge(kq_loaded, 128 * h)
                    act.activation(ks[:, :], bank[4][0:TS, 0:DK], ACT.Copy, scale=cst[0:TS, C_KDS + h:C_KDS + h + 1])\
                        .then_inc(bank_read[4], 1)
                    await_read(act, 4, *step)
                    act.activation(ks_hi[:, :], ks[:, :], ACT.Copy).then_inc(ks_hi_done, 1)
                elif kind == "OP":
                    h = step[1]
                    if h:
                        act.wait_ge(y_lo_done, h)
                    else:
                        act.wait_ge(x_lo_done, KT)
                    for n in range(2):
                        await_full(act, 6 + n, *step)
                        act.activation(scr[:, 2 * n:2 * n + 2, 0:TP], bank[6 + n][:, :].rearrange("p (e i) -> p e i", e=2),
                                       ACT.Copy).then_inc(bank_read[6 + n], 1)
                elif kind == "SF":
                    h = step[1]
                    if h:
                        act.wait_ge(fin_stored, 16 * h)
                    for d in range(2):
                        await_full(act, 3 + d, *step)
                        act.activation(fin[:, d, :], bank[3 + d][:, :], ACT.Copy).then_inc(bank_read[3 + d], 1)
                elif kind == "GNA":
                    h = step[1]
                    await_full(act, 5, "OSI", h)
                    act.activation(scr[:, 0:4, TP:T], bank[5][:, 0:4 * TS].rearrange("p (e i) -> p e i", e=4), ACT.Copy)\
                        .then_inc(bank_read[5], 1)
                    await_read(act, 5, "OSI", h)
                    if h:
                        await_full(act, 4, "SS", h - 1)
                    act.activation(scr[:, 4:8, :], scr[:, 0:4, :], ACT.Square).then_inc(sq_done, 1)
                elif kind == "SS":
                    h = step[1]
                    await_full(act, 4, *step)
                    act.activation(rsb[:, :], bank[4][:, 0:T], ACT.Sqrt, bias=eps[:, 0:1], scale=1.0 / DV)\
                        .then_inc(bank_read[4], 1)
                    act.wait_ge(y_done, h + 1)
                    if h >= 2:
                        await_full(act, *tile_use("ro", 8 * (h - 2) + 7))
                    act.activation(ym_hi[:, 4 * (h % 2):4 * (h % 2) + 4, :], scr[:, 0:4, :], ACT.Copy).then_inc(y_hi_done, 1)
                elif kind == "BT":
                    await_full(act, 6, *step)
                elif kind == "QR":
                    await_full(act, 7, "QSS")
                    act.activation(rsq[:, :], bank[7][:, 0:20], ACT.Sqrt, bias=eps[:, 1:2]).then_inc(bank_read[7], 1)
                elif kind == "KP":
                    n = step[1]
                    await_full(act, 4, *step)
                    await_ks(act, n - 2)
                    act.activation(ktc[:, n % 2, 4:8, :], bank[4][:, :].rearrange("p (h k) -> p h k", h=4), ACT.Copy)\
                        .then_inc(bank_read[4], 1)
                elif kind == "KS" and step[1] % 4 == 3:
                    pair = step[1] // 4
                    await_full(act, 5, "ST", pair)
                    act.activation(sst[:, pair, :], bank[5][:, 0:2 * P], ACT.Copy).then_inc(bank_read[5], 1)
                elif kind == "KX":
                    await_full(act, 7, *step)
                    act.activation(mkT[:, 2 * step[1] + 1, :], bank[7][:, 0:T], ACT.Copy).then_inc(bank_read[7], 1)
                elif kind == "SA":
                    p = step[1]
                    act.wait_ge(sa_max, p + 1)
                    act.activation(ps[:, p % 2, :], ps[:, p % 2, :], ACT.Exp, bias=nmxs[:, p:p + 1],
                                   accum_out=dens[:, p:p + 1]).then_inc(sa_exp, 1)
                elif kind == "SB":
                    p = step[1]
                    await_full(act, 6, *step)
                    act.activation(pts[:, p, :], bank[6][:, 0:PAST], ACT.Copy)
                    act.activation(ptn[:, p, :], bank[6][0:TS, PAST:PAST + P], ACT.Copy).then_inc(bank_read[6], 1)
                elif kind == "A":
                    h = step[1]
                    act.wait_ge(a_max, h + 1)
                    for n, cols in enumerate((slice(0, TP), slice(TP, TP + P))):
                        ins = act.activation(pp[:, h % 2, cols], pp[:, h % 2, cols], ACT.Exp, bias=nmx[:, h % 2, n:n + 1],
                                             accum_out=den[:, h % 2, n:n + 1])
                    ins.then_inc(a_exp, 1)
                elif kind == "B":
                    h = step[1]
                    await_full(act, 4, *step)
                    if h >= 2:
                        await_full(act, 6, "C", h - 2)
                    act.activation(pt[:, h % 2, :], bank[4][:, 0:TP + P], ACT.Copy).then_inc(bank_read[4], 1)
                elif kind == "C":
                    h = step[1]
                    await_read(act, 6, *step)
                    if h == 0:
                        await_full(act, *tile_use("mv", 11))
                    act.activation(xn_hi[:, h, 0:TP], yf[:, h % 2, :], ACT.Copy).then_inc(x_hi_done, 1)
                elif kind == "PG":
                    await_read(act, 7, "OSM")
                    act.activation(xn_hi[:, :, TP:T], yfs[:, :, :], ACT.Copy).then_inc(x_hi_done, 1)

        @block.vector
        def _(dve):
            done = Steps(dve, dve_steps)

            def split_lo(c):
                if c >= nchunks:
                    return
                dve.wait_ge(w_hi_done, c + 1)
                dve.tensor_tensor(w_lo[:, c % 2, :], w_raw[:, c % RAW, :], w_hi[:, c % 2, :].bitcast(F32), ALU.subtract)\
                    .then_inc(w_lo_done, 1)

            def mask_keys(s):
                h, b = s // NSEQ, s % NSEQ
                if b == 0:
                    dve.wait_ge(kq_loaded, 128 * (h + 1))
                if s >= 2:
                    await_full(dve, 7, "U", (s - 2) // NSEQ, (s - 2) % NSEQ)
                dve.tensor_scalar(km[:, s % 2, :], kq[:, b // 4, :].bitcast(F32),
                                  cst[:, C_QM + b % 4:C_QM + b % 4 + 1], None, ALU.mult).then_inc(km_done, 1)

            def normed(kt, col):
                dve.scalar_tensor_tensor(scr[:, kt, :], xT[:, kt, :], wcols[:, col + kt:col + kt + 1], rsb[:, :],
                                         ALU.mult, ALU.mult).then_inc(unsplit_done, 1)

            nx = 0
            nk = 0
            for step in steps:
                kind = step[0]
                if kind == "CHUNK":
                    split_lo(step[1] + 1)
                elif kind == "X":
                    for kt in range(KT):
                        await_full(dve, kt, "X", kt)
                        if kt == 0:
                            done(dve.tensor_copy(wcols[:, 0:41], bank[0][:, 384:425]))
                        dve.tensor_copy(xT[:, kt, :], bank[kt][:, 0:T]).then_inc(bank_read[kt], 1)
                elif kind == "NORM":
                    w = step[1]
                    if w == 0:
                        split_lo(0)
                    await_read(dve, 7, *step)
                    done(dve.reciprocal(rsb[:, :], rsb[:, :]))
                    done.wait()
                    for n in range(2 if w else 1):
                        hi, lo = (ym_hi, ym_lo) if w and n == 0 else (xn_hi, xn_lo)
                        col = (W_MOBA if n == 0 else W_KV) if w else W_RET
                        for kt in range(KT + 1):
                            if kt < KT:
                                if n:
                                    dve.wait_ge(x_lo_done, KT + kt + 1)
                                normed(kt, col)
                            if kt:
                                nx += 1
                                dve.wait_ge(x_hi_done, nx)
                                dve.tensor_tensor(lo[:, kt - 1, :], scr[:, kt - 1, :], hi[:, kt - 1, :].bitcast(F32),
                                                  ALU.subtract).then_inc(x_lo_done, 1)
                elif kind == "TILE":
                    c, i, b = step[1:]
                    what, h, part = chunks[c]
                    if what == "ro":
                        n = 4 * part + i
                        await_full(dve, b, *step[:3])
                        if h:
                            await_read(dve, *tile_use("ro", 8 * (h - 1) + n))
                        dve.tensor_tensor(xT[:, n, :], xT[:, n, :], bank[b][:, 0:T], ALU.add).then_inc(bank_read[b], 1)
                    elif what == "mk":
                        m = TOK[i][1]
                        dve.wait_ge(kss_done, nk + 1)
                        done(dve.reciprocal(kss[0:m, nk % 2, :], kss[0:m, nk % 2, :]))
                        done.wait()
                        if h >= 2:
                            dve.wait_ge(rows_stored[h % 2], 48)
                            await_full(dve, 7, "KX", h - 2)
                        for d in range(2):
                            ins = dve.scalar_tensor_tensor(rows[0:m, h % 2, i, P * d:P * d + P], bank[b][0:m, P * d:P * d + P],
                                                           kss[0:m, nk % 2, d:d + 1], knw[0:m, :], ALU.mult, ALU.mult)
                        ins.then_inc(bank_read[b], 1)
                        nk += 1
                    elif what == "mo" and (3 * h + i) % 2:
                        await_full(dve, b, *step[:3])
                        dve.wait_ge(rows_stored[h % 2], 48 * (2 + h // 2))
                        dve.tensor_copy(rows[0:TOK[i][1], h % 2, i, :], bank[b][0:TOK[i][1], 0:256]).then_inc(bank_read[b], 1)
                elif kind == "SC":
                    h = step[1]
                    await_full(dve, 5, *step)
                    if h == 0:
                        dve.wait_ge(cst_loaded, 16)
                    else:
                        await_full(dve, 7, "OP", h - 1)
                        dve.wait_ge(osi_done, h)
                    dt = cst[:, C_DT + TP * h:C_DT + TP * h + TP]
                    dve.tensor_tensor(sT[:, 0:TP], bank[5][:, 0:TP], dt, ALU.mult)
                    dve.tensor_tensor(sT[:, TP:TP + P], bank[5][:, TP:TP + P], dt[:, 0:P], ALU.mult)
                    dve.tensor_tensor(s2[:, :], bank[5][0:TS, TP + P:TP + P + TS],
                                      cst[0:TS, C_DS + TS * h:C_DS + TS * h + TS], ALU.mult).then_inc(bank_read[5], 1)
                elif kind == "U":
                    h, b = step[1:]
                    s = NSEQ * h + b
                    if b == 0:
                        mask_keys(s)
                    if b < NSEQ - 1:
                        mask_keys(s + 1)
                    for d in range(2):
                        await_full(dve, 6 + d, *step)
                        half = st[:, s % NST, DV * d:DV * d + DV]
                        dve.scalar_tensor_tensor(half, half, math.exp(NEW * LOG_DECAY[h]), bank[6 + d][:, :],
                                                 ALU.mult, ALU.add).then_inc(bank_read[6 + d], 1)
                elif kind == "SS":
                    h = step[1]
                    await_read(dve, 4, *step)
                    done(dve.reciprocal(rsb[:, :], rsb[:, :]))
                    done.wait()
                    for e in range(4):
                        w = wcols[:, W_GN + 4 * h + e:W_GN + 4 * h + e + 1]
                        done(dve.scalar_tensor_tensor(scr[:, e, :], scr[:, e, :], w, rsb[:, :], ALU.mult, ALU.mult))
                    done.wait()
                    for i in range(4 * h, 4 * h + 4):
                        await_read(dve, *tile_use("rg", i))
                    dve.tensor_tensor(scr[:, 0:4, :], scr[:, 0:4, :], gs[:, h % 2, :, :], ALU.mult).then_inc(y_done, 1)
                    dve.wait_ge(y_hi_done, h + 1)
                    dst = slice(4 * (h % 2), 4 * (h % 2) + 4)
                    dve.tensor_tensor(ym_lo[:, dst, :], scr[:, 0:4, :], ym_hi[:, dst, :].bitcast(F32), ALU.subtract)\
                        .then_inc(y_lo_done, 1)
                elif kind == "BT":
                    await_full(dve, 6, *step)
                    done(dve.memset(line[:, :], MASKED))
                    done.wait()
                    dve.tensor_copy(line[:, 0:FAR + 1], bank[6][0:MH, 0:FAR + 1]).then_inc(bank_read[6], 1)
                elif kind == "QR":
                    await_read(dve, 7, "QSS")
                    done(dve.reciprocal(rsq[:, :], rsq[:, :]))
                    done.wait()
                elif kind == "KP":
                    n = step[1]
                    await_full(dve, 3, *step)
                    await_ks(dve, n - 2)
                    dve.tensor_copy(ktc[:, n % 2, 0:4, :], bank[3][:, :].rearrange("p (h k) -> p h k", h=4))\
                        .then_inc(bank_read[3], 1)
                elif kind == "KX":
                    await_full(dve, 6, *step)
                    dve.tensor_copy(mkT[:, 2 * step[1], :], bank[6][:, 0:T]).then_inc(bank_read[6], 1)
                elif kind == "SN":
                    await_full(dve, 6, *step)
                    dve.tensor_copy(sstn[:, :], bank[6][0:TS, :]).then_inc(bank_read[6], 1)
                elif kind == "SA":
                    p = step[1]
                    if p == 0:
                        dve.wait_ge(bias_loaded, 16 * 11)
                    await_full(dve, 5, *step)
                    if p >= 2:
                        await_full(dve, 6, "SB", p - 2)
                    r = rsq[:, 16 + p:17 + p]
                    dve.scalar_tensor_tensor(ps[:, p % 2, 0:PAST], bank[5][:, 0:PAST], r, bs[:, :], ALU.mult, ALU.add)
                    dve.scalar_tensor_tensor(ps[:, p % 2, PAST:T], bank[5][:, PAST:T], r, bn[:, p, :], ALU.mult, ALU.add)\
                        .then_inc(bank_read[5], 1)
                    await_read(dve, 5, *step)
                    dve.tensor_reduce(nmxs[:, p:p + 1], ps[:, p % 2, :], AX.X, ALU.max, negate=True).then_inc(sa_max, 1)
                    dve.wait_ge(sa_exp, p + 1)
                    done(dve.reciprocal(dens[:, p:p + 1], dens[:, p:p + 1]))
                    done.wait()
                    dve.tensor_scalar(ps[:, p % 2, :], ps[:, p % 2, :], dens[:, p:p + 1], None, ALU.mult).then_inc(sa_done, 1)
                elif kind == "A":
                    h = step[1]
                    await_full(dve, 3, *step)
                    if h >= 2:
                        await_full(dve, 4, "B", h - 2)
                    dve.scalar_tensor_tensor(pp[:, h % 2, 0:TP], bank[3][:, 0:TP], rsq[:, 2 * h + 1:2 * h + 2], tb[:, h, :],
                                             ALU.mult, ALU.add)
                    dve.scalar_tensor_tensor(pp[:, h % 2, TP:TP + P], bank[3][:, TP:TP + P], rsq[:, 2 * h:2 * h + 1],
                                             tb[:, h, P:TP], ALU.mult, ALU.add).then_inc(bank_read[3], 1)
                    await_read(dve, 3, *step)
                    dve.tensor_reduce(nmx[:, h % 2, 0:1], pp[:, h % 2, 0:TP], AX.X, ALU.max, negate=True)
                    dve.tensor_reduce(nmx[:, h % 2, 1:2], pp[:, h % 2, TP:TP + P], AX.X, ALU.max, negate=True).then_inc(a_max, 1)
                    dve.wait_ge(a_exp, h + 1)
                    done(dve.reciprocal(den[:, h % 2, :], den[:, h % 2, :]))
                    done.wait()
                    dve.tensor_scalar(pp[:, h % 2, 0:TP], pp[:, h % 2, 0:TP], den[:, h % 2, 0:1], None, ALU.mult)
                    dve.tensor_scalar(pp[:, h % 2, TP:TP + P], pp[:, h % 2, TP:TP + P], den[:, h % 2, 1:2], None, ALU.mult)\
                        .then_inc(a_done, 1)
                elif kind == "C":
                    h = step[1]
                    await_full(dve, 6, *step)
                    await_read(dve, *tile_use("mg", h))
                    dve.tensor_tensor(yf[:, h % 2, :], bank[6][:, 0:TP], scr[:, h, 0:TP], ALU.mult).then_inc(bank_read[6], 1)
                    dve.wait_ge(x_hi_done, 24 + h + 1 + (h == MH - 1))
                    dve.tensor_tensor(xn_lo[:, h, 0:TP], yf[:, h % 2, :], xn_hi[:, h, 0:TP].bitcast(F32), ALU.subtract)\
                        .then_inc(x_lo_done, 1)
                elif kind == "PG":
                    await_full(dve, 7, "OSM")
                    await_read(dve, *tile_use("mg", MH - 1))
                    dve.tensor_tensor(yfs[:, :, :], bank[7][:, :].rearrange("p (h i) -> p h i", h=MH), scr[:, :, TP:T],
                                      ALU.mult).then_inc(bank_read[7], 1)
                    dve.wait_ge(x_hi_done, 24 + MH)
                    dve.tensor_tensor(xn_lo[:, :, TP:T], yfs[:, :, :], xn_hi[:, :, TP:T].bitcast(F32), ALU.subtract)\
                        .then_inc(x_lo_done, 1)

        @block.gpsimd
        def _(pool):
            done = Steps(pool, pool_steps)
            done(pool.memset(eps[:, 0:1], EPS))
            done.wait()
            pool.memset(eps[:, 1:2], EPS * HD).then_inc(eps_done, 1)
            cos, sin = cst[:, C_COS:C_COS + T], cst[:, C_SIN:C_SIN + T]
            for step in steps:
                kind = step[0]
                if kind == "TILE" and chunks[step[1]][0] in ("rq", "rk") and step[2] == 1:
                    c, i, b = step[1:]
                    what, h, _ = chunks[c]
                    qk = int(what == "rk")
                    if h == 0 and qk == 0:
                        pool.wait_ge(cst_loaded, 16)
                    for n in range(2):
                        await_read(pool, *tile_use(what, 2 * h + n))
                    if h:
                        await_full(pool, 5, "SC", h - 1)
                    if h >= 2 and not qk:
                        await_full(pool, 7, "U", h - 2, NSEQ - 1)
                    x1, x2, dst = raw_qk[:, qk, 0, :], raw_qk[:, qk, 1, :], (qT, kT)[qk]
                    if done.n > 1:
                        done.wait()
                    for n, (x, tab) in enumerate(((x1, cos), (x2, sin), (x1, sin), (x2, cos))):
                        done(pool.tensor_tensor(rt[:, n, :], x, tab, ALU.mult))
                    done.wait()
                    done(pool.tensor_tensor(dst[:, 0, :], rt[:, 0, :], rt[:, 1, :], ALU.subtract))
                    ins = pool.tensor_tensor(dst[:, 1, :], rt[:, 2, :], rt[:, 3, :], ALU.add)
                    if not qk:
                        done(ins)
                        done.wait()
                        dec = cst[:, C_QD + TS * h:C_QD + TS * h + TS]
                        done(pool.tensor_tensor(qd[:, h % 2, 0, :], qT[:, 0, TP:T], dec, ALU.mult))
                        ins = pool.tensor_tensor(qd[:, h % 2, 1, :], qT[:, 1, TP:T], dec, ALU.mult)
                    ins.then_inc(rot_done, 1)
                    pool.wait_ge(rot_done, 2 * h + qk + 1)
                elif kind == "TILE" and chunks[step[1]][0] == "rv" and step[2] == 2:
                    h, part = chunks[step[1]][1:]
                    cols = slice(256 * part, 256 * part + 256)
                    pool.wait_ge(vs_hi_done, 2 * h + part + 1)
                    pool.tensor_tensor(vs_lo[:, cols], vs[:, cols], vs_hi[:, cols].bitcast(F32), ALU.subtract)\
                        .then_inc(vs_lo_done, 1)
                elif kind == "KT":
                    pool.wait_ge(ks_hi_done, step[1] + 1)
                    pool.tensor_tensor(ks_lo[:, :], ks[:, :], ks_hi[:, :].bitcast(F32), ALU.subtract).then_inc(ks_lo_done, 1)
                elif kind == "BT":
                    await_full(pool, 6, *step)
                    pool.memset(bn[:, :, :], MASKED).then_inc(bn_masked, 1)


_OUTS = [("y_prompt", (1, TP, D)), ("y_sample", (NSEQ, NEW, D)),
         ("ret_state_prompt", (1, 1, RH, DK, DV)), ("ret_state_sample", (1, NSEQ, RH, DK, DV)),
         ("k_prompt", (1, TP, MH, HD)), ("v_prompt", (1, TP, MH, HD)),
         ("k_sample", (NSEQ, NEW, MH, HD)), ("v_sample", (NSEQ, NEW, MH, HD))]


def kernel(**inputs):
    import concourse.bacc as bacc
    from concourse.bass_utils import run_bass_kernel_spmd

    nc = bacc.Bacc("TRN2", target_bir_lowering=False, num_devices=1)
    arrays, aps = {}, {}
    given = {name: np.ascontiguousarray(v) for name, v in inputs.items()}
    given["c_ret"], given["c_eye"], given["c_hot"] = shape_constants()
    for name, v in given.items():
        arrays[f"in_{name}"] = v
        aps[name] = nc.dram_tensor(f"in_{name}", v.shape, mybir.dt.from_np(v.dtype), kind="ExternalInput").ap()
    for name, shape in _OUTS:
        aps[name] = nc.dram_tensor(f"out_{name}", shape, F32, kind="ExternalOutput").ap()
    build(nc, aps)
    r = run_bass_kernel_spmd(nc, [arrays], core_ids=[0])
    return tuple(r.results[0][f"out_{name}"] for name, _ in _OUTS)
```

```python
import math
from contextlib import ExitStack

import numpy as np

import concourse.bass as bass
from concourse import mybir

F32 = mybir.dt.float32
F32R = mybir.dt.float32r
I32 = mybir.dt.int32
ALU = mybir.AluOpType
ACT = mybir.ActivationFunctionType
AX = mybir.AxisListType

P = 128
D = 1024
KT = D // P
TP, TS = 256, 64
T = TP + TS
NSEQ, NEW = 8, 8
RH, DK, DV = 4, 256, 512
MH, HD = 8, 128
PAST, PAGE = 256, 128
NPG = PAST // PAGE
EPS = 1e-6
MASKED = -1e30
BUCKETS, MAX_DIST = 32, 128
CW = 2048
RAW = 3
NST = 5
NCP = 4
FAR = PAST + NEW - 1
LINE = 392
TOK = [(0, P), (P, P), (TP, TS)]

TILES = {"rq": 2, "rk": 2, "rv": 3, "rg": 2, "ro": 4, "mq": 2, "mk": 3, "mv": 3, "mg": 2, "mo": 3}

LOG_DECAY = [math.log1p(-(2.0 ** (-5 - h))) for h in range(RH)]

C_COS, C_SIN = 0, T
C_DS = 2 * T
C_QD = C_DS + RH * TS
C_KDP = C_QD + RH * TS
C_KDS = C_KDP + 2 * RH
C_QM = C_KDS + RH
C_SEL = C_QM + 4
C_SB = C_SEL + TS
C_DT = C_SB
C_N = C_DT + RH * TP


def shape_constants():
    half = DK // 2
    inv = np.float32(10000.0) ** (-np.arange(half, dtype=np.float32) / half)
    pos = np.concatenate([np.arange(TP), PAST + np.tile(np.arange(NEW), NSEQ)]).astype(np.float32)
    ang = (pos[None, :] * inv[:, None].astype(np.float32)).astype(np.float32).astype(np.float64)
    lg = np.array(LOG_DECAY)
    scale = DK ** -0.5
    c = np.zeros((P, C_N))
    c[:, C_COS:C_COS + T] = np.cos(ang)
    c[:, C_SIN:C_SIN + T] = np.sin(ang)
    j, i = np.arange(P)[:, None, None], np.arange(TP)[None, None, :]
    c[:, C_DT:C_N] = np.where(i >= j, np.exp(lg[None, :, None] * np.maximum(i - j, 0)) * scale, 0).reshape(P, -1)
    t = np.arange(TS)
    same = (t[:, None] // NEW == t[None, :] // NEW) & (t[None, :] >= t[:, None])
    gap = np.maximum(t[None, :] - t[:, None], 0)
    c[:TS, C_DS:C_QD] = (np.where(same, 1, 0)[:, None, :] * np.exp(lg[None, :, None] * gap[:, None, :]) * scale).reshape(TS, -1)
    c[:, C_QD:C_KDP] = np.exp((t % NEW + 1)[None, :] * lg[:, None]).reshape(1, -1)
    for tile in range(2):
        tok = tile * P + np.arange(P)
        c[:, C_KDP + tile * RH:C_KDP + (tile + 1) * RH] = np.exp((TP - 1 - tok)[:, None] * lg[None, :]) * scale
    c[:TS, C_KDS:C_KDS + RH] = np.exp((NEW - 1 - t % NEW)[:, None] * lg[None, :]) * scale
    c[:, C_QM:C_QM + 4] = (np.arange(P)[:, None] % 32) // NEW == np.arange(4)[None, :]
    row = np.arange(P)
    c[:, C_SEL:C_SB] = (row // TS * 32 + row % 32)[:, None] == np.arange(TS)[None, :]
    eye = np.concatenate([np.eye(P), np.ones((P, P))], axis=1)
    dist = FAR - np.arange(FAR + 1)
    exact = BUCKETS // 2
    n = np.maximum(dist, 1).astype(np.float32)
    big = exact + (np.log(n / np.float32(exact)) / np.float32(math.log(MAX_DIST / exact))
                   * np.float32(BUCKETS - exact)).astype(np.int32)
    bucket = np.where(dist < exact, dist, np.minimum(big, BUCKETS - 1))
    hot = (bucket[None, :] == np.arange(BUCKETS)[:, None])
    return c.astype(np.float32), eye.astype(np.float32), hot.astype(np.float32)


def make_schedule():
    chunks, steps, use, used = [], [], {}, [0] * 8

    def fill(bank, *key):
        use[(*key, bank)] = used[bank]
        used[bank] += 1

    tiles = [0]

    def chunk(kind, a, b, gaps):
        c = len(chunks)
        chunks.append((kind, a, b))
        steps.append(("CHUNK", c))
        for i in range(TILES[kind]):
            j = tiles[0]
            tiles[0] += 1
            fill(j % 3, "TILE", c, i)
            steps.append(("TILE", c, i, j % 3))
            for s in gaps[i] if i < len(gaps) else []:
                add(*s)
        steps.append(("ENDCHUNK", c))

    banks = {"KT": (3, 4), "SC": (5,), "OP": (6, 7), "SF": (3, 4), "OSI": (5,), "FX": (5,), "U": (6, 7), "SS": (5,), "SR": (), "SG": (), "SM": (),
             "GNA": (), "SH": (), "BT": (6,), "NORM": (7,), "QS": (), "QSS": (7,), "QR": (), "KP": (3, 4), "KS": (),
             "KX": (6, 7), "SN": (6,), "SA": (5,), "SB": (6,), "OSM": (7,), "PG": (),
             "A": (3,), "B": (4,), "C": (6,), "W": (), "SQ": (), "NS": (), "RMS": (), "ME": (), "NB": (),
             "ST": (), "PN": ()}

    def add(*s):
        for b in banks[s[0]]:
            fill(b, *s)
        if s[0] == "U" and s[2] % 4 == 0:
            fill(5, "UR", s[1], s[2] // 4)
        steps.append(s)

    def states(h, b0, b1):
        return [[("U", h, b)] for b in range(b0, b1)]

    for kt in range(KT):
        fill(kt, "X", kt)
    steps.append(("X",))
    steps.append(("NORM", 0))
    for h in range(RH):
        u = states(h - 1, 0, 8) if h else [[]] * 8
        tail = [[("FX", h - 1), ("GNA", h - 1), ("SG", h - 1)], [("SS", h - 1)]] if h else [[], []]
        if h in (1, 2):
            tail[1] += [("SR", h - 1), ("SM", h - 1)]
        chunk("rq", h, 0, u[0:2] if h else [[], [("ST", 0)]])
        chunk("rk", h, 0, u[2:4])
        chunk("rv", h, 0, u[4:7])
        chunk("rv", h, 1, [u[7]] + tail)
        if h == 3:
            chunk("ro", 0, 0, [[("SR", 2)], [], [("SM", 2)]])
            chunk("ro", 0, 1, [])
        chunk("rg", h, 0, [[("KT", h)], [("SC", h)] + ([("SH", h - 1)] if h else [])])
        chunk("rg", h, 1, [[("OP", h)], [("SF", h), ("OSI", h)]])
    u = states(3, 0, 8)
    g = [[] for _ in range(16)]
    for n, at in enumerate((0, 1, 2, 3, 4, 5, 6, 7)):
        g[at] += u[n]
    for n, step in enumerate(([("FX", 3), ("GNA", 3), ("SG", 3)], [("SS", 3)], [("SR", 3)], [("SM", 3)], [("SH", 3)])):
        g[8 + n] += step
    for n in range(4):
        chunk("ro", 1 + n // 2, n % 2, g[4 * n:4 * n + 4])
    fill(7, "NORM", 1)
    g = [([("SQ", n - 1)] if n else []) + ([("W", n - 1)] if 1 <= n <= 4 else []) + ([("NS", n - 2)] if n >= 2 else [])
         for n in range(KT)]
    g[1].append(("BT",))
    chunk("ro", 3, 0, g[0:4])
    chunk("ro", 3, 1, g[4:8])
    for n in range(4, KT):
        add("W", n)
    add("SQ", KT - 1)
    fill(7, "QSS")
    g = [[("ME", n)] + ([("QS", n - 2)] if n >= 2 else []) for n in range(MH)]
    g[0] = [("NS", KT - 2), ("NS", KT - 1), ("RMS",), ("ME", 0)]
    for kt in range(KT + 1):
        g[1 + (kt + 1) // 2].append(("NB", kt))
    g[6].append(("ST", 1))
    for c in range(4):
        chunk("mq", c, 0, g[2 * c:2 * c + 2])
    kp = []
    for n in range(NSEQ * NPG):
        lag = [("KS", n - 1)] if n else []
        kp.append([("KP", n)] + lag)
        if n % 4 == 0:
            fill(5, "PS", n // 4)
    kp.append([("KS", 15)])
    kp[0] += [("QS", 6)]
    kp[1] += [("QS", 7), ("QR",)]
    for c in range(4):
        g = kp[3 * c:3 * c + 3]
        chunk("mk", c, 0, [g[0] + ([("KX", c - 1)] if c else []), g[1], g[2]])
    chunk("mv", 0, 0, [kp[12] + [("KX", 3)], kp[13], kp[14]])
    chunk("mv", 1, 0, [kp[15], kp[16] + [("SN",)], [("SA", 0)]])
    chunk("mv", 2, 0, [[("SA", 1), ("SB", 0)], [("SA", 2), ("SB", 1)], [("SA", 3), ("SB", 2)]])
    chunk("mv", 3, 0, [[("SB", 3), ("A", 0)], [("A", 1), ("B", 0)], [("A", 2), ("B", 1), ("PN",)]])
    fill(7, "OSM")
    for c in range(4):
        g = []
        for i in (2 * c, 2 * c + 1):
            s = ([("A", i + 3)] if i + 3 < MH else []) + ([("B", i + 2)] if i + 2 < MH else []) + [("C", i)]
            if i == 7:
                s += [("PG",), ("ST", 2)]
            g.append(s)
        chunk("mg", c, 0, g)
    for c in range(4):
        chunk("mo", c, 0, [])
    return chunks, steps, use


def build(nc, a):
    chunks, steps, use = make_schedule()
    nchunks = len(chunks)
    ctx = ExitStack()
    with ctx:
        def sb(name, shape, dt=F32, stack=ctx):
            return stack.enter_context(nc.sbuf_tensor(name, shape, dt))

        def sem(name):
            return ctx.enter_context(nc.semaphore(name))

        w_raw = sb("w_raw", [P, RAW, CW])
        w_hi = sb("w_hi", [P, 2, CW], F32R)
        w_lo = sb("w_lo", [P, 2, CW], F32R)
        xT = sb("xT", [P, KT, T])
        xn_hi = sb("xn_hi", [P, KT, T + TS], F32R)
        xn_lo = sb("xn_lo", [P, KT, T], F32R)
        ym_hi = sb("ym_hi", [P, KT, T], F32R)
        ym_lo = sb("ym_lo", [P, KT, T], F32R)
        scr = sb("scr", [P, KT, T])
        eye = sb("eye", [P, 2 * P])
        ident, ones = eye[:, 0:P], eye[:, P:2 * P]
        wcols = sb("wcols", [P, 48])
        eps = sb("eps", [P, 2])
        rsb = sb("rsb", [P, T])
        rms = sb("rms", [P, 4])
        half = sb("half", [TS, 256])
        W_RET, W_KV, W_MOBA, W_GN, W_Q = 0, 8, 16, 24, 40

        ret = ExitStack()
        def rb(name, shape, dt=F32):
            return sb(name, shape, dt, ret)
        st = rb("st", [P, NST, 2 * DV])
        cst = rb("cst", [P, C_SB])
        dt = rb("dt", [P, TP])
        wrow = rb("wrow", [41, P])
        raw_qk = rb("raw_qk", [P, 2, 2, T])
        rt = rb("rt", [P, 2, T])
        qT = rb("qT", [P, 2, T])
        kT = rb("kT", [P, 2, T])
        qd = rb("qd", [P, 2, TS])
        qdm = rb("qdm", [P, 2, NSEQ, TS], F32R)
        st_hi = rb("st_hi", [P, 2, DV], F32R)
        st_lo = rb("st_lo", [P, 2, DV], F32R)
        cross = scr.ap().rearrange("p k t -> p (k t)")[:, 4 * T:4 * T + DV]
        vp = rb("vp", [P, 2, DV])
        vs = rb("vs", [TS, DV])
        vs_hi = rb("vs_hi", [TS, DV], F32R)
        vs_lo = rb("vs_lo", [TS, DV], F32R)
        vq = rb("vq", [P, 2, DV], F32R)
        kd = rb("kd", [P, 2, DK])
        ks = rb("ks", [TS, DK])
        ks_hi = rb("ks_hi", [TS, DK], F32R)
        ks_lo = rb("ks_lo", [TS, DK], F32R)
        kq = rb("kq", [P, 2, DK], F32R)
        km = rb("km", [P, 2, DK], F32R)
        gs = rb("gs", [P, 4, T])
        diag = gs.ap().rearrange("p e t -> p (e t)")[:, 0:3 * P].rearrange("p (t i) -> p t i", t=3)
        sT = rb("sT", [P, TP + P])
        s2 = rb("s2", [TS, TS])
        fin = rb("fin", [P, 2, DV])
        ret.close()

        moba = ExitStack()
        def mb(name, shape, dt=F32):
            return sb(name, shape, dt, moba)
        cache = mb("cache", [P, NCP, D])
        mkT = mb("mkT", [P, MH, T])
        mqT = mb("mqT", [P, MH, T])
        mvp = mb("mvp", [P, 2, D])
        mvs = mb("mvs", [TS, D])
        rows = mb("rows", [P, 2, 3, 256])
        ktc = mb("ktc", [P, 2, MH, P])
        tb = mb("tb", [P, MH, TP])
        bs = mb("bs", [P, PAST])
        bn = mb("bn", [P, 4, TS])
        sst = mb("sst", [P, 4, 2 * P])
        sstn = mb("sstn", [TS, 4 * P])
        ps = mb("ps", [P, 2, T])
        pts, ptn = sst, sstn.ap().rearrange("j (s k) -> j s k", s=4)
        free = ktc.ap().rearrange("p s h k -> p s (h k)")[:, :, 0:2 * (TP + P)]
        pp = free[:, 0, :].rearrange("p (s k) -> p s k", s=2)
        pt = free[:, 1, :].rearrange("p (s k) -> p s k", s=2)
        sqs = mb("sqs", [P, NSEQ, MH, NEW])
        sqp = mb("sqp", [P, 2, TP])
        yf, yfs = sqp, sqs.ap().rearrange("p b h t -> p (b h t)").rearrange("p (h i) -> p h i", h=MH)
        junk = mb("junk", [P, P])
        knw = mb("knw", [P, HD])
        hot = sst.ap().rearrange("p s k -> p (s k)")[0:BUCKETS, 0:FAR + 1]
        relb = mb("relb", [BUCKETS, MH])
        line = sstn[0:MH, 0:LINE]
        pages = mb("pages", [1, NSEQ * NPG], I32)
        rsq = mb("rsq", [P, 20])
        kss = mb("kss", [P, 2, 2])
        nmx = mb("nmx", [P, 2, 2])
        den = mb("den", [P, 2, 2])
        nmxs = mb("nmxs", [P, 4])
        dens = mb("dens", [P, 4])
        moba.close()

        bank = [ctx.enter_context(nc.psum_tensor(f"bank{i}", [P, 512], F32)) for i in range(8)]
        scratch = nc.dram_tensor("bias_lines", (P, MH, LINE), F32, kind="Internal").ap()

        x_loaded = [sem(f"x_loaded{t}") for t in range(3)]
        const_loaded, cst_loaded = sem("const_loaded"), sem("cst_loaded")
        roots_done, diag_done, rms_done = sem("roots_done"), sem("diag_done"), sem("rms_done")
        w_loaded = [sem(f"w_loaded{i}") for i in range(RAW)]
        w_hi_done, w_lo_done = sem("w_hi_done"), sem("w_lo_done")
        bank_full = [sem(f"bank_full{i}") for i in range(8)]
        bank_read = [sem(f"bank_read{i}") for i in range(8)]
        eps_done = sem("eps_done")
        sq_done = sem("sq_done")
        unsplit_done = sem("unsplit_done")
        x_hi_done, x_lo_done = sem("x_hi_done"), sem("x_lo_done")
        rot_done = sem("rot_done")
        vs_hi_done, vs_lo_done = sem("vs_hi_done"), sem("vs_lo_done")
        ks_hi_done, ks_lo_done = sem("ks_hi_done"), sem("ks_lo_done")
        vq_loaded, kq_loaded, km_done = sem("vq_loaded"), sem("kq_loaded"), sem("km_done")
        dt_loaded = sem("dt_loaded")
        qd_hi_done, qd_lo_done = sem("qd_hi_done"), sem("qd_lo_done")
        st_hi_done, st_lo_done = sem("st_hi_done"), sem("st_lo_done")
        cross_done = sem("cross_done")
        gated_done = sem("gated_done")
        y_done, y_hi_done, y_lo_done = sem("y_done"), sem("y_hi_done"), sem("y_lo_done")
        fin_stored = sem("fin_stored")
        st_loaded = [sem(f"st_loaded{i}") for i in range(NST)]
        st_stored = [sem(f"st_stored{i}") for i in range(NST)]
        act_steps, dve_steps, pool_steps = sem("act_steps"), sem("dve_steps"), sem("pool_steps")
        moba_loaded, pages_loaded = sem("moba_loaded"), sem("pages_loaded")
        line_stored, bias_loaded, bn_masked = sem("line_stored"), sem("bias_loaded"), sem("bn_masked")
        qs_done = sem("qs_done")
        cache_loaded = [sem(f"cache_loaded{i}") for i in range(NCP)]
        ks_done = sem("ks_done")
        pv_done = sem("pv_done")
        kss_done = sem("kss_done")
        rows_stored = [sem("rows_stored0"), sem("rows_stored1")]
        sa_max, sa_exp, sa_done = sem("sa_max"), sem("sa_exp"), sem("sa_done")
        a_max, a_exp, a_done = sem("a_max"), sem("a_exp"), sem("a_done")
        half_done, sum_done = sem("half_done"), sem("sum_done")
        stack_done = sem("stack_done")
        q_done, gate_done = sem("q_done"), sem("gate_done")
        stored = sem("stored")

        class Steps:
            def __init__(self, eng, s):
                self.eng, self.s, self.n = eng, s, 0

            def __call__(self, ins):
                ins.then_inc(self.s, 1)
                self.n += 1

            def wait(self):
                self.eng.wait_ge(self.s, self.n)

        def await_free(pe, b, *key):
            if use[(*key, b)]:
                pe.wait_ge(bank_read[b], use[(*key, b)])

        def await_full(eng, b, *key):
            eng.wait_ge(bank_full[b], use[(*key, b)] + 1)

        def await_read(eng, b, *key):
            eng.wait_ge(bank_read[b], use[(*key, b)] + 1)

        def await_ks(eng, n):
            if n < 0:
                return
            if n % 4 == 3:
                await_full(eng, 5, "PS", n // 4)
            else:
                eng.wait_ge(ks_done, n + 1 - (n + 1) // 4)

        def await_cross(eng, s):
            h, b = s // NSEQ, s % NSEQ
            if b % 4 == 3:
                await_full(eng, 5, "UR", h, b // 4)
            else:
                eng.wait_ge(cross_done, 6 * h + b + 1 - b // 4)

        def qdm_at(j, low):
            col = 32 * low + NEW * j
            return qdm[:, :, :, :].rearrange("p d (g j) m -> p (d g) j m", j=4)[:, :, j, col:col + NEW]

        def qd_at(j):
            return qd[:, :, :].rearrange("p d (g m) -> p (d g) m", m=32)[:, :, NEW * j:NEW * j + NEW]

        def tile_use(kind, i):
            c = [k for k, x in enumerate(chunks) if x[0] == kind][i // TILES[kind]]
            return next((s[3], *s[:3]) for s in steps if s[:3] == ("TILE", c, i % TILES[kind]))

        def last_tile(c):
            return next((s[3], *s[:3]) for s in steps if s[:3] == ("TILE", c, TILES[chunks[c][0]] - 1))

        t2 = [(s[3], *s[:3]) for s in steps if s[0] == "TILE" and s[2] == 2 and chunks[s[1]][0] in ("rv", "mk", "mv", "mo")]

        def chunk_source(c):
            kind, h, i = chunks[c]
            if kind[0] == "r" and kind != "ro":
                col = {"rq": h * DK, "rk": RH * DK + h * DK, "rv": 2 * RH * DK + h * DV + i * 256,
                       "rg": 2 * RH * DK + RH * DV + h * DV + i * 256}[kind]
                return a["ret_w_in"][0].rearrange("(k p) n -> p k n", p=P)[:, :, col:col + 256]
            if kind == "ro":
                return a["ret_w_out"][0].rearrange("(k p) n -> p k n", p=P)[:, 4 * h:4 * h + 4, 512 * i:512 * i + 512]
            src, off = {"mq": (a["moba_w_in"][0], 0), "mg": (a["moba_w_in"][0], D), "mk": (a["w_kv"], 0),
                        "mv": (a["w_kv"], D), "mo": (a["moba_w_out"][0], 0)}[kind]
            return src.rearrange("(k p) n -> p k n", p=P)[:, :, off + 256 * h:off + 256 * h + 256]

        def chunk_view(buf, c, s):
            n = 512 if chunks[c][0] == "ro" else 256
            return buf[:, s, :].rearrange("p (k n) -> p k n", n=n)

        st_dram = a["state_ret"][0].rearrange("b h (k p) e -> b h p k e", p=P)
        st_out = a["ret_state_sample"][0].rearrange("b h (k p) e -> b h p k e", p=P)
        x_rows = [a["x_prompt"][0, 0:P], a["x_prompt"][0, P:TP], a["x_sample"].rearrange("b t d -> (b t) d")]

        def out_rows(name):
            p, s = a[f"{name}_prompt"], a[f"{name}_sample"]
            if name != "y":
                p, s = p.rearrange("b t h d -> b t (h d)"), s.rearrange("b t h d -> b t (h d)")
            return [p[0, 0:P], p[0, P:TP], s.rearrange("b t d -> (b t) d")]

        k_out, v_out, y_out = out_rows("k"), out_rows("v"), out_rows("y")
        block = ctx.enter_context(nc.Block())

        @block.sync
        def _(sp):
            n_stored = [0]

            def store(dst, src):
                sp.dma_start(dst, src).then_inc(stored, 16)
                n_stored[0] += 16

            def load_chunk(c):
                if c >= nchunks:
                    return
                if c >= RAW:
                    sp.wait_ge(w_lo_done, 2 * (c - RAW + 1))
                sp.dma_start(chunk_view(w_raw, c, c % RAW), chunk_source(c)).then_inc(w_loaded[c % RAW], 16)

            def load_state(s):
                if s >= RH * NSEQ:
                    return
                if s >= NST:
                    sp.wait_ge(st_stored[s % NST], 16 * (s // NST))
                elif s < 3:
                    await_full(sp, KT - 1, "X", KT - 1)
                    sp.wait_ge(roots_done, 2)
                sp.dma_start(st[:, s % NST, :].rearrange("p (k e) -> p k e", k=2),
                             st_dram[s % NSEQ, s // NSEQ]).then_inc(st_loaded[s % NST], 16)

            def store_state(s):
                await_read(sp, 6, "U", s // NSEQ, s % NSEQ)
                await_read(sp, 7, "U", s // NSEQ, s % NSEQ)
                sp.dma_start(st_out[s % NSEQ, s // NSEQ],
                             st[:, s % NST, :].rearrange("p (k e) -> p k e", k=2)).then_inc(st_stored[s % NST], 16)

            def load_page(n):
                m, vals = n % 16, n >= 16
                if n >= 16 + NCP:
                    sp.wait_ge(pv_done, n - 15 - NCP)
                elif n >= NCP:
                    await_full(sp, 4, "KP", n - NCP)
                page = sp.value_load(pages[0:1, m:m + 1], min_val=0, max_val=a["cache_k"].shape[0] - 1)
                src = a["cache_v"] if vals else a["cache_k"]
                sp.dma_start(cache[:, n % NCP, :], src[bass.ds(page, 1)].rearrange("o p h d -> p (o h d)"))\
                    .then_inc(cache_loaded[n % NCP], 16)

            sp.dma_start(eye[:, :], a["c_eye"]).then_inc(const_loaded, 16)
            for t, (c0, m) in enumerate(TOK):
                sp.dma_start(st[0:m, t, :], x_rows[t]).then_inc(x_loaded[t], 16)
            for r0, name, n in ((W_RET, "ret_norm_w", 8), (W_KV, "kv_norm_w", 8), (W_MOBA, "moba_norm_w", 8),
                                (W_GN, "ret_gn_w", 16), (W_Q, "q_norm_w", 1)):
                v = a[name]
                v = {1: lambda: v, 2: lambda: v.rearrange("a n -> (a n)"),
                     3: lambda: v.rearrange("a h n -> (a h n)")}[len(v.shape)]()
                sp.dma_start(wrow[r0:r0 + n, :], v.rearrange("(r p) -> r p", p=P)).then_inc(const_loaded, 16)
            load_chunk(0)
            sp.dma_start(cst[:, :], a["c_ret"][:, 0:C_SB]).then_inc(cst_loaded, 16)
            load_chunk(1)
            sp.dma_start(dt[:, :], a["c_ret"][:, C_DT:C_DT + TP]).then_inc(dt_loaded, 16)

            for step in steps:
                kind = step[0]
                if kind == "CHUNK":
                    c = step[1]
                    load_chunk(c + 2)
                    if c == 2:
                        for s in range(3):
                            load_state(s)
                elif kind == "KT":
                    h = step[1]
                    sp.wait_ge(vs_lo_done, 2 * (h + 1))
                    if h:
                        await_full(sp, 7, "U", h - 1, NSEQ - 1)
                    for g in range(2):
                        for term, src in enumerate((vs_hi, vs_lo, vs_hi, vs_lo)):
                            sp.dma_start(vq[32 * term:32 * term + 32, g, :].bitcast(F32), src[32 * g:32 * g + 32, :].bitcast(F32))\
                                .then_inc(vq_loaded, 16)
                elif kind == "SC":
                    h = step[1]
                    sp.wait_ge(ks_lo_done, h + 1)
                    if h:
                        sp.wait_ge(km_done, NSEQ * h)
                    for g in range(2):
                        for term, src in enumerate((ks_hi, ks_hi, ks_lo, ks_lo)):
                            sp.dma_start(kq[32 * term:32 * term + 32, g, :].bitcast(F32), src[32 * g:32 * g + 32, :].bitcast(F32))\
                                .then_inc(kq_loaded, 16)
                elif kind == "OP" and step[1] < RH - 1:
                    h = step[1]
                    await_read(sp, 5, "SC", h)
                    sp.dma_start(dt[:, :], a["c_ret"][:, C_DT + TP * (h + 1):C_DT + TP * (h + 2)]).then_inc(dt_loaded, 16)
                elif kind == "U":
                    s = step[1] * NSEQ + step[2]
                    if s:
                        store_state(s - 1)
                    load_state(s + 3)
                    if step[2] == 1:
                        await_read(sp, 3, "SF", step[1])
                        await_read(sp, 4, "SF", step[1])
                        sp.dma_start(a["ret_state_prompt"][0, 0, step[1]].rearrange("(k p) e -> p k e", p=P),
                                     fin[:, :, :]).then_inc(fin_stored, 16)
                elif kind == "BT":
                    store_state(RH * NSEQ - 1)
                    for s in range(RH * NSEQ - NST, RH * NSEQ):
                        sp.wait_ge(st_stored[s % NST], 16 * (s // NST + 1))
                    sp.wait_ge(fin_stored, 16 * RH)
                    sp.wait_ge(y_lo_done, RH)
                    sp.dma_start(hot[:, :], a["c_hot"]).then_inc(moba_loaded, 16)
                    sp.dma_start(relb[:, :], a["rel_bias"]).then_inc(moba_loaded, 16)
                    sp.dma_start(knw[:, :], bass.AP(a["k_norm_w"].tensor, 0, [[0, P], [1, HD]])).then_inc(moba_loaded, 16)
                    sp.dma_start(pages[:, :], a["page_table"].rearrange("b n -> (b n)").rearrange("(o n) -> o n", o=1))\
                        .then_inc(pages_loaded, 16)
                elif kind == "NS" and step[1] == 0:
                    await_read(sp, 6, "BT")
                    sp.dma_start(scratch.rearrange("r h u -> h r u"),
                                 line[:, :].rearrange("h (o u) -> h o u", o=1).broadcast_to((MH, P, LINE)))\
                        .then_inc(line_stored, 16)
                elif kind == "ME" and 1 <= step[1] <= NCP:
                    if step[1] == 1:
                        sp.wait_ge(pages_loaded, 16)
                    load_page(step[1] - 1)
                elif kind == "KP":
                    n = step[1]
                    if 1 <= n <= 12:
                        load_page(n + 3)
                    lines, skew = scratch.tensor, MH * LINE - 1
                    if n == 5:
                        sp.wait_ge(line_stored, 16)
                        for b2 in range(2):
                            sp.dma_start(bs[TS * b2:TS * b2 + TS, :],
                                         bass.AP(lines, FAR - PAST, [[LINE, MH], [skew, NEW], [1, PAST]])).then_inc(bias_loaded, 16)
                    if n in (6, 7, 8, 9):
                        if n == 6:
                            sp.wait_ge(bn_masked, 1)
                        pair = n - 6
                        for b2 in range(2):
                            c0 = (2 * pair + b2) * NEW
                            sp.dma_start(bn[TS * b2:TS * b2 + TS, pair, c0:c0 + NEW],
                                         bass.AP(lines, FAR, [[LINE, MH], [skew, NEW], [1, NEW]])).then_inc(bias_loaded, 16)
                    if n == 10:
                        sp.dma_start(tb[:, :, :], bass.AP(lines, FAR - P, [[skew, P], [LINE, MH], [1, TP]])).then_inc(bias_loaded, 16)
                elif kind == "KX":
                    c = step[1]
                    for t in range(3):
                        await_read(sp, *tile_use("mk", 3 * c + t))
                    for t, (c0, m) in enumerate(TOK):
                        sp.dma_start(k_out[t][:, 256 * c:256 * c + 256], rows[0:m, c % 2, t, :])\
                            .then_inc(rows_stored[c % 2], 16)
                elif kind == "SN":
                    for n in range(16, 20):
                        load_page(n)
                elif kind == "TILE" and chunks[step[1]][0] == "mg":
                    g = 2 * chunks[step[1]][1] + step[2]
                    if g < 6:
                        load_page(20 + 2 * g)
                        load_page(21 + 2 * g)
                elif kind == "A" and step[1] == 3:
                    for t in range(3):
                        await_read(sp, *tile_use("mv", 9 + t))
                    for t, (c0, m) in enumerate(TOK):
                        store(v_out[t], mvp[:, t, :] if t < 2 else mvs[:, :])
                elif kind == "ENDCHUNK" and chunks[step[1]][0] == "mo":
                    c = chunks[step[1]][1]
                    for t, (c0, m) in enumerate(TOK):
                        await_read(sp, *tile_use("mo", 3 * c + t))
                        sp.dma_start(y_out[t][:, 256 * c:256 * c + 256], rows[0:m, c % 2, t, :])\
                            .then_inc(rows_stored[c % 2], 16)
            for s in range(RH * NSEQ - NST, RH * NSEQ):
                sp.wait_ge(st_stored[s % NST], 16 * (s // NST + 1))
            sp.wait_ge(fin_stored, 16 * RH)
            for r in rows_stored:
                sp.wait_ge(r, 4 * 48)
            sp.wait_ge(stored, n_stored[0])

        @block.tensor
        def _(pe):
            def close(mm, b):
                mm.then_inc(bank_full[b], 1)

            def page_values(n, h):
                b, pg = n // 2, n % 2
                if h == 0:
                    pe.wait_ge(cache_loaded[n % NCP], 16 * ((16 + n) // NCP + 1))
                col = P * pg + TS * (b % 2) + NEW * h
                mm = pe.matmul(bank[7][:, TS * h + NEW * b:TS * h + NEW * b + NEW], cache[:, n % NCP, P * h:P * h + P],
                               pts[:, b // 2, col:col + NEW], start=False, stop=n == 15 and h == MH - 1, skip_group_check=True)
                if n == 15 and h == MH - 1:
                    close(mm, 7)
                elif h == MH - 1:
                    mm.then_inc(pv_done, 1)

            def project(step):
                _, c, i, b = step
                kind, h, part = chunks[c]
                tiles = [(i, b)]
                if c == 0:
                    if i == 1:
                        return
                    tiles = [(0, b), (1, tile_use("rq", 1)[0])]
                    await_free(pe, *tile_use("rq", 1))
                if i == 0:
                    pe.wait_ge(w_lo_done, 2 * c + 1)
                await_free(pe, b, "TILE", c, i)
                hi, lo = chunk_view(w_hi, c, c % 2), chunk_view(w_lo, c, c % 2)
                x_hi, x_lo, k0, nk = xn_hi[:, :, 0:T], xn_lo, 0, KT
                if kind in ("mq", "mg"):
                    x_hi, x_lo = ym_hi, ym_lo
                if kind == "ro":
                    x_hi, x_lo, k0, nk = ym_hi, ym_lo, 4 * (h % 2), 4
                    if i == 0 and part == 0:
                        pe.wait_ge(y_lo_done, h + 1)
                first = {"rq": 8, "mq": 16, "mk": 24, "mo": 32}.get(kind) if h == 0 and i == 0 and part == 0 else None
                stacked = kind in ("rv", "mk", "mv", "mo") and i == 2
                if stacked and h == 0 and part == 0:
                    pe.wait_ge(stack_done, {"rv": 1, "mk": 2, "mv": 2, "mo": 3}[kind])
                for k in range(nk):
                    if i == 0 and k == nk // 2:
                        pe.wait_ge(w_lo_done, 2 * c + 2)
                    if stacked:
                        for n, w in enumerate((hi, lo)):
                            mm = pe.matmul(bank[b][:, 0:256], xn_hi[:, k, TP:T + TS], w[:, k, :],
                                           start=k == 0 and n == 0, stop=k == nk - 1 and n == 1)
                        continue
                    if first:
                        pe.wait_ge(x_lo_done, first - 8 + k + 1)
                    for n, (w, x) in enumerate(((hi, x_hi), (hi, x_lo), (lo, x_hi))):
                        flags = {"start": k == 0 and n == 0, "stop": k == nk - 1 and n == 2 and kind != "mo"}
                        if kind in ("rv", "mk", "mv", "mo"):
                            c0, m = TOK[i]
                            mm = pe.matmul(bank[b][0:m, 0:256], x[:, k, c0:c0 + m], w[:, k, :], **flags)
                            continue
                        for tile, out in tiles:
                            mm = pe.matmul(bank[out][:, 0:T], w[:, k, P * tile:P * tile + P], x[:, k0 + k, :], **flags)
                            if flags["stop"]:
                                close(mm, out)
                    if kind == "mg":
                        for n in range(2):
                            page_values(2 * (2 * h + i) + k // 4, 2 * (k % 4) + n)
                if kind == "mo":
                    c0, m = TOK[i]
                    for k in range(2):
                        mm = pe.matmul(bank[b][0:m, P * k:P * k + P], xT[:, 2 * h + k, c0:c0 + m], ident,
                                       start=False, stop=k == 1, skip_group_check=stacked)
                if kind in ("rv", "mk", "mv", "mo"):
                    close(mm, b)

            for step in steps:
                kind = step[0]
                if kind == "X":
                    for t in range(3):
                        pe.wait_ge(x_loaded[t], 16)
                    pe.wait_ge(const_loaded, 16 * 6)
                    for kt in range(KT):
                        if kt == 5:
                            pe.wait_ge(diag_done, 1)
                            for t, (c0, m) in enumerate(TOK):
                                mm = pe.matmul(bank[1 + t][:, 384:384 + m], ones[0:m, :], diag[0:m, t, 0:m],
                                               start=True, stop=True)
                            mm.then_inc(rms_done, 1)
                        for t, (c0, m) in enumerate(TOK):
                            mm = pe.transpose(bank[kt][:, c0:c0 + m], st[0:m, t, P * kt:P * kt + P], ident[0:m, 0:m])
                        if kt == 0:
                            mm = pe.transpose(bank[0][:, 384:425], wrow[:, :], ident[0:41, 0:41])
                        close(mm, kt)
                elif kind == "NS":
                    kt = step[1]
                    if kt == 0:
                        await_free(pe, 7, "NORM", 1)
                    pe.wait_ge(sq_done, RH + kt + 1)
                    mm = pe.matmul(bank[7][:, 0:T], ones, scr[:, kt, :], start=kt == 0, stop=kt == KT - 1)
                    if kt == KT - 1:
                        close(mm, 7)
                elif kind == "TILE":
                    project(step)
                elif kind == "ENDCHUNK":
                    pass
                elif kind == "KT":
                    h = step[1]
                    pe.wait_ge(rot_done, 2 * (h + 1))
                    await_free(pe, 3, *step)
                    for t in range(2):
                        for d in range(2):
                            mm = pe.transpose(bank[3][:, DK * t + P * d:DK * t + P * d + P], kT[:, d, P * t:P * t + P], ident)
                    close(mm, 3)
                    await_free(pe, 4, *step)
                    for d in range(2):
                        mm = pe.transpose(bank[4][0:TS, P * d:P * d + P], kT[:, d, TP:T], ident)
                    close(mm, 4)
                elif kind == "SC":
                    await_free(pe, 5, *step)
                    for col, n, j, m, i0 in ((0, TP, 0, P, 0), (TP, P, P, P, P), (TP + P, TS, TP, TS, TP)):
                        for d in range(2):
                            mm = pe.matmul(bank[5][0:m, col:col + n], kT[:, d, j:j + m], qT[:, d, i0:i0 + n],
                                           start=d == 0, stop=d == 1)
                    close(mm, 5)
                elif kind == "OP":
                    h = step[1]
                    await_read(pe, 5, "SC", h)
                    for i in range(6 * h, 6 * h + 6):
                        await_read(pe, *tile_use("rv", i))
                    for e in range(4):
                        b = 6 + e // 2
                        if e % 2 == 0:
                            await_free(pe, b, *step)
                        o = bank[b][:, TP * (e % 2):TP * (e % 2) + TP]
                        pe.matmul(o, vp[:, 0, P * e:P * e + P], sT[:, 0:TP], start=True, stop=False)
                        mm = pe.matmul(o[:, P:TP], vp[:, 1, P * e:P * e + P], sT[:, TP:TP + P], start=False, stop=True)
                        if e % 2:
                            close(mm, b)
                elif kind == "SF":
                    await_read(pe, 3, "KT", step[1])
                    for d in range(2):
                        await_free(pe, 3 + d, *step)
                        for t in range(2):
                            mm = pe.matmul(bank[3 + d][:, :], kd[:, t, P * d:P * d + P], vp[:, t, :],
                                           start=t == 0, stop=t == 1)
                        close(mm, 3 + d)
                elif kind == "OSI":
                    await_free(pe, 5, *step)
                    for e in range(4):
                        mm = pe.matmul(bank[5][:, TS * e:TS * e + TS], vs[:, P * e:P * e + P], s2[:, :],
                                       start=True, stop=True)
                    close(mm, 5)
                elif kind == "U":
                    h, b = step[1:]
                    s = NSEQ * h + b
                    if b == 0:
                        pe.wait_ge(qd_lo_done, h + 1)
                    if b % 4 == 0:
                        await_free(pe, 5, "UR", h, b // 4)
                    for d in range(2):
                        pe.wait_ge(st_lo_done, 2 * s + d + 1)
                        for n, w in enumerate((st_hi, st_lo)):
                            mm = pe.matmul(bank[5][0:TS, :], qdm[:, d, b, :], w[:, d, :],
                                           start=b % 4 == 0 and d == 0 and n == 0, stop=b % 4 == 3 and d == 1 and n == 1)
                    if b % 4 == 3:
                        close(mm, 5)
                    else:
                        mm.then_inc(cross_done, 1)
                    if b == 0:
                        pe.wait_ge(vq_loaded, 128 * (h + 1))
                    pe.wait_ge(km_done, s + 1)
                    for d in range(2):
                        await_free(pe, 6 + d, *step)
                        close(pe.matmul(bank[6 + d][:, :], km[:, s % 2, P * d:P * d + P], vq[:, b // 4, :],
                                        start=True, stop=True), 6 + d)
                elif kind == "FX":
                    await_free(pe, 5, *step)
                    for e in range(4):
                        mm = pe.matmul(bank[5][:, TS * e:TS * e + TS], cross[:, P * e:P * e + P], cst[:, C_SEL:C_SEL + TS],
                                       start=True, stop=True)
                    close(mm, 5)
                elif kind == "SS":
                    pe.wait_ge(sq_done, step[1] + 1)
                    await_free(pe, 5, *step)
                    for e in range(4):
                        mm = pe.matmul(bank[5][:, 0:T], ones, scr[:, 4 + e, :], start=e == 0, stop=e == 3)
                    close(mm, 5)
                elif kind == "BT":
                    pe.wait_ge(moba_loaded, 48)
                    await_free(pe, 6, *step)
                    close(pe.matmul(bank[6][0:MH, 0:FAR + 1], relb[:, :], hot[:, :], start=True, stop=True), 6)
                elif kind == "QS":
                    h = step[1]
                    pe.wait_ge(q_done, h + 1)
                    if h == 0:
                        await_free(pe, 7, "QSS")
                    for t in range(2):
                        mm = pe.matmul(bank[7][:, 2 * h + t:2 * h + t + 1], sqp[:, h % 2, P * t:P * t + P], ones[:, 0:1],
                                       start=True, stop=True)
                    if h < MH - 1:
                        mm.then_inc(qs_done, 1)
                    else:
                        for pair in range(4):
                            mm = pe.matmul(bank[7][:, 16 + pair:17 + pair],
                                           sqs[:, 2 * pair:2 * pair + 2].rearrange("p b h t -> p (b h t)"), ones[:, 0:1],
                                           start=True, stop=True)
                        close(mm, 7)
                elif kind == "KP":
                    n = step[1]
                    pe.wait_ge(cache_loaded[n % NCP], 16 * (n // NCP + 1))
                    for h in range(MH):
                        b = 3 + h // 4
                        if h % 4 == 0:
                            await_free(pe, b, *step)
                        mm = pe.transpose(bank[b][:, P * (h % 4):P * (h % 4) + P], cache[:, n % NCP, P * h:P * h + P], ident)
                        if h % 4 == 3:
                            close(mm, b)
                elif kind == "KS":
                    n = step[1]
                    b, pg = n // 2, n % 2
                    await_read(pe, 3, "KP", n)
                    await_read(pe, 4, "KP", n)
                    if n % 4 == 0:
                        await_free(pe, 5, "PS", n // 4)
                    for h in range(MH):
                        col = P * pg + TS * (b % 2) + NEW * h
                        mm = pe.matmul(bank[5][:, col:col + NEW], ktc[:, n % 2, h, :], mqT[:, h, TP + NEW * b:TP + NEW * b + NEW],
                                       start=True, stop=True)
                    if n % 4 == 3:
                        close(mm, 5)
                    else:
                        mm.then_inc(ks_done, 1)
                elif kind == "KX":
                    c = step[1]
                    for t in range(3):
                        await_read(pe, *tile_use("mk", 3 * c + t))
                    for i in range(2):
                        await_free(pe, 6 + i, *step)
                        for t, (c0, m) in enumerate(TOK):
                            mm = pe.transpose(bank[6 + i][:, c0:c0 + m], rows[0:m, c % 2, t, P * i:P * i + P], ident[0:m, 0:m])
                        close(mm, 6 + i)
                elif kind == "SN":
                    await_free(pe, 6, *step)
                    await_read(pe, 6, "KX", 3)
                    await_read(pe, 7, "KX", 3)
                    o = bank[6][0:TS, :].rearrange("p (b h t) -> p b h t", b=NSEQ, h=MH)
                    for h in range(MH):
                        mm = pe.matmul(o[:, :, h, :], mkT[:, h, TP:T], mqT[:, h, TP:T], start=True, stop=True)
                    close(mm, 6)
                elif kind == "SA":
                    pair = step[1]
                    if pair == 0:
                        await_read(pe, 5, "PS", 3)
                        await_read(pe, 6, "SN")
                    await_free(pe, 5, *step)
                    for pg in range(2):
                        pe.transpose(bank[5][:, P * pg:P * pg + P], sst[:, pair, P * pg:P * pg + P], ident)
                    close(pe.transpose(bank[5][:, PAST:PAST + TS], sstn[:, P * pair:P * pair + P], ident[0:TS, 0:TS]), 5)
                elif kind == "SB":
                    pair = step[1]
                    pe.wait_ge(sa_done, pair + 1)
                    await_free(pe, 6, *step)
                    for pg in range(2):
                        pe.transpose(bank[6][:, P * pg:P * pg + P], ps[:, pair % 2, P * pg:P * pg + P], ident)
                    close(pe.transpose(bank[6][0:TS, PAST:PAST + P], ps[:, pair % 2, PAST:T], ident), 6)
                elif kind == "PN":
                    await_free(pe, 7, "OSM")
                    await_read(pe, 6, "SB", 3)
                    await_read(pe, *tile_use("mv", 11))
                    new = ptn.rearrange("j s (c h t) -> j (s c) h t", c=2, t=NEW)
                    for h in range(MH):
                        pe.matmul(bank[7][:, TS * h:TS * h + TS], mvs[:, P * h:P * h + P], new[:, :, h, :],
                                  start=h == 0, stop=False, skip_group_check=True)
                elif kind == "A":
                    h = step[1]
                    if h == 0:
                        await_read(pe, 6, "KX", 3)
                        await_read(pe, 7, "KX", 3)
                    await_free(pe, 3, *step)
                    pe.matmul(bank[3][:, 0:TP], mqT[:, h, P:TP], mkT[:, h, 0:TP], start=True, stop=True)
                    close(pe.matmul(bank[3][:, TP:TP + P], mqT[:, h, 0:P], mkT[:, h, 0:P], start=True, stop=True), 3)
                elif kind == "B":
                    h = step[1]
                    pe.wait_ge(a_done, h + 1)
                    await_free(pe, 4, *step)
                    for i, col in enumerate((TP, 0, P)):
                        mm = pe.transpose(bank[4][:, P * i:P * i + P], pp[:, h % 2, col:col + P], ident)
                    close(mm, 4)
                elif kind == "C":
                    h = step[1]
                    await_read(pe, 4, "B", h)
                    await_free(pe, 6, *step)
                    pe.matmul(bank[6][:, 0:TP], mvp[:, 0, P * h:P * h + P], pt[:, h % 2, 0:TP], start=True, stop=False)
                    close(pe.matmul(bank[6][:, P:TP], mvp[:, 1, P * h:P * h + P], pt[:, h % 2, TP:TP + P],
                                    start=False, stop=True), 6)

        @block.scalar
        def _(act):
            done = Steps(act, act_steps)

            n_half = [0]

            def lower_half(c, b):
                if n_half[0]:
                    await_read(act, *t2[n_half[0] - 1])
                n_half[0] += 1
                act.activation(half[:, :], bank[b][TS:P, 0:256], ACT.Copy).then_inc(half_done, 1)

            def split_hi(c, halves=(0, 1)):
                if c >= nchunks:
                    return
                act.wait_ge(w_loaded[c % RAW], 16 * (c // RAW + 1))
                if c >= 2:
                    await_full(act, *last_tile(c - 2))
                for n in halves:
                    half_w = slice(CW // 2 * n, CW // 2 * (n + 1))
                    act.activation(w_hi[:, c % 2, half_w], w_raw[:, c % RAW, half_w], ACT.Copy).then_inc(w_hi_done, 1)

            act.wait_ge(eps_done, 1)
            nk = 0
            def state_hi(s):
                act.wait_ge(st_loaded[s % NST], 16 * (s // NST + 1))
                if s:
                    await_cross(act, s - 1)
                for d in range(2):
                    act.activation(st_hi[:, d, :], st[:, s % NST, DV * d:DV * d + DV], ACT.Copy).then_inc(st_hi_done, 1)

            for step in steps:
                kind = step[0]
                if kind == "CHUNK":
                    split_hi(step[1] + 1)
                elif kind == "ENDCHUNK" and chunks[step[1]] == ("rg", 0, 1):
                    state_hi(0)
                elif kind == "U":
                    h, b = step[1:]
                    s = NSEQ * h + b
                    if b % 4 == 3:
                        await_full(act, 5, "UR", h, b // 4)
                        rows_at = slice(TS * (b // 4), TS * (b // 4) + TS)
                        act.activation(cross[rows_at, :], bank[5][0:TS, :], ACT.Copy).then_inc(bank_read[5], 1)
                    if s + 1 < RH * NSEQ:
                        state_hi(s + 1)
                elif kind == "OSI":
                    await_full(act, 5, *step)
                    act.activation(scr[:, 0:4, TP:T], bank[5][:, 0:4 * TS].rearrange("p (e i) -> p e i", e=4), ACT.Copy)\
                        .then_inc(bank_read[5], 1)
                elif kind == "W":
                    kt = step[1]
                    await_read(act, *tile_use("ro", 24 + kt))
                    if kt == 0:
                        await_full(act, *tile_use("ro", 23))
                    if kt == 4:
                        await_full(act, *tile_use("ro", 31))
                    act.activation(ym_hi[:, kt, :], xT[:, kt, :], ACT.Copy, scale=wcols[:, W_MOBA + kt:W_MOBA + kt + 1])\
                        .then_inc(x_hi_done, 1)
                elif kind == "SQ":
                    kt = step[1]
                    await_read(act, *tile_use("ro", 24 + kt))
                    if kt == 0:
                        act.wait_ge(y_lo_done, RH)
                    act.activation(scr[:, kt, :], xT[:, kt, :], ACT.Square).then_inc(sq_done, 1)
                elif kind == "RMS":
                    await_full(act, 7, "NORM", 1)
                    act.activation(rsb[:, :], bank[7][:, 0:T], ACT.Sqrt, bias=eps[:, 0:1], scale=1.0 / D)\
                        .then_inc(bank_read[7], 1)
                elif kind == "NB":
                    kt = step[1]
                    if kt == KT:
                        continue
                    if kt == 0:
                        await_full(act, *tile_use("rg", 15))
                    act.wait_ge(unsplit_done, KT + kt + 1)
                    act.activation(xn_hi[:, kt, 0:T], scr[:, kt, :], ACT.Copy).then_inc(x_hi_done, 1)
                elif kind == "ST":
                    n = step[1]
                    act.wait_ge(x_lo_done, (8, 24, 24 + MH + 1)[n])
                    if n:
                        await_full(act, *tile_use(*(("rv", 23), ("mv", 11))[n - 1]))
                    act.activation(xn_hi[:, :, T:T + TS], xn_lo[:, :, TP:T].bitcast(F32), ACT.Copy).then_inc(stack_done, 1)
                elif kind == "ME":
                    head = step[1]
                    await_read(act, *tile_use("mq", head))
                    if head >= 2:
                        act.wait_ge(qs_done, head - 1)
                    act.activation(sqp[:, head % 2, :], ps[:, head % 2, 0:TP], ACT.Square)
                    act.activation(sqs[:, :, head, :], ps[:, head % 2, TP:T].rearrange("p (b t) -> p b t", t=NEW), ACT.Square)
                    act.activation(mqT[:, head, :], ps[:, head % 2, :], ACT.Copy, scale=wcols[:, W_Q:W_Q + 1])\
                        .then_inc(q_done, 1)
                elif kind == "X":
                    done(act.activation(rms[:, 3:4], eps[:, 0:1], ACT.Sqrt))
                    flat = scr.ap().rearrange("p k t -> p (k t)")
                    for t, (c0, m) in enumerate(TOK):
                        act.wait_ge(x_loaded[t], 16)
                        if t == 2:
                            done.wait()
                        done(act.activation(flat[0:m, D * (t % 2):D * (t % 2) + D], st[0:m, t, :], ACT.Square,
                                            accum_out=rms[0:m, t:t + 1]))
                    done.wait()
                    act.activation(rms[:, 0:2], rms[:, 0:2], ACT.Sqrt, bias=eps[:, 0:1], scale=1.0 / D).then_inc(roots_done, 1)
                    act.activation(rms[0:TS, 2:3], rms[0:TS, 2:3], ACT.Sqrt, bias=eps[0:TS, 0:1], scale=1.0 / D)\
                        .then_inc(roots_done, 1)
                elif kind == "NORM":
                    split_hi(0, (0,))
                    for kt in range(KT):
                        act.wait_ge(unsplit_done, kt + 1)
                        act.activation(xn_hi[:, kt, 0:T], scr[:, kt, :], ACT.Copy).then_inc(x_hi_done, 1)
                        if kt == 1:
                            split_hi(0, (1,))
                        act.activation(xT[:, kt, :], bank[kt][:, 0:T], ACT.Copy).then_inc(bank_read[kt], 1)
                elif kind == "TILE":
                    c, i, b = step[1:]
                    what, h, part = chunks[c]
                    if what in ("ro", "mq"):
                        continue
                    if what == "mo" and i == 1:
                        continue
                    if what == "mg":
                        await_read(act, b, *step[:3])
                        act.activation(scr[:, 2 * h + i, :], scr[:, 2 * h + i, :], ACT.Silu).then_inc(gate_done, 1)
                        continue
                    await_full(act, b, *step[:3])
                    if i == 2:
                        lower_half(c, b)
                    if what in ("rq", "rk"):
                        qk = int(what == "rk")
                        if h:
                            act.wait_ge(rot_done, 2 * h - 1 + qk)
                        act.activation(raw_qk[:, qk, i, :], bank[b][:, 0:T], ACT.Copy).then_inc(bank_read[b], 1)
                    elif what == "rv" and i < 2:
                        if h:
                            await_full(act, 4, "SF", h - 1)
                        act.activation(vp[:, i, 256 * part:256 * part + 256], bank[b][:, 0:256], ACT.Copy)\
                            .then_inc(bank_read[b], 1)
                    elif what == "rv":
                        cols = slice(256 * part, 256 * part + 256)
                        if h:
                            act.wait_ge(vs_lo_done, 2 * h)
                            act.wait_ge(vq_loaded, 128 * h)
                        await_read(act, b, *step[:3])
                        act.activation(vs_hi[:, cols], vs[:, cols], ACT.Copy).then_inc(vs_hi_done, 1)
                    elif what == "rg":
                        if h:
                            act.wait_ge(gated_done, h)
                        act.activation(gs[:, 2 * part + i, :], bank[b][:, 0:T], ACT.Silu).then_inc(bank_read[b], 1)
                    elif what == "mk":
                        m = TOK[i][1]
                        src = bank[b]
                        if i == 2:
                            src = half
                            act.wait_ge(sum_done, h + 1)
                        if nk >= 2:
                            await_read(act, *tile_use("mk", nk - 2))
                        for d in range(2):
                            if nk or d:
                                done.wait()
                            done(act.activation(junk[0:m, :], src[0:m, P * d:P * d + P], ACT.Square,
                                                accum_out=kss[0:m, nk % 2, d:d + 1]))
                        done.wait()
                        act.activation(kss[0:m, nk % 2, :], kss[0:m, nk % 2, :], ACT.Sqrt, bias=eps[0:m, 0:1], scale=1.0 / HD)\
                            .then_inc(kss_done, 1)
                        nk += 1
                    elif what == "mv" and i < 2:
                        act.activation(mvp[:, i, 256 * h:256 * h + 256], bank[b][:, 0:256], ACT.Copy).then_inc(bank_read[b], 1)
                    elif what == "mo" and i < 2:
                        act.wait_ge(rows_stored[h % 2], 48 * (2 + h // 2))
                        act.activation(rows[0:TOK[i][1], h % 2, i, :], bank[b][0:TOK[i][1], 0:256], ACT.Copy)\
                            .then_inc(bank_read[b], 1)
                elif kind == "KT":
                    h = step[1]
                    await_full(act, 3, *step)
                    if h:
                        await_full(act, 4, "SF", h - 1)
                    for t in range(2):
                        ins = act.activation(kd[:, t, :], bank[3][:, DK * t:DK * t + DK], ACT.Copy,
                                             scale=cst[:, C_KDP + RH * t + h:C_KDP + RH * t + h + 1])
                    ins.then_inc(bank_read[3], 1)
                    await_full(act, 4, *step)
                    if h:
                        act.wait_ge(ks_lo_done, h)
                        act.wait_ge(kq_loaded, 128 * h)
                    act.activation(ks[:, :], bank[4][0:TS, 0:DK], ACT.Copy, scale=cst[0:TS, C_KDS + h:C_KDS + h + 1])\
                        .then_inc(bank_read[4], 1)
                    await_read(act, 4, *step)
                    act.activation(ks_hi[:, :], ks[:, :], ACT.Copy).then_inc(ks_hi_done, 1)
                    if h:
                        await_full(act, 5, "UR", h - 1, 1)
                    for j in range(4):
                        ins = act.activation(qdm_at(j, 0), qd_at(j), ACT.Copy)
                    ins.then_inc(qd_hi_done, 1)
                elif kind == "OP":
                    h = step[1]
                    if h:
                        act.wait_ge(y_lo_done, h)
                    else:
                        act.wait_ge(x_lo_done, KT)
                    for n in range(2):
                        await_full(act, 6 + n, *step)
                        act.activation(scr[:, 2 * n:2 * n + 2, 0:TP], bank[6 + n][:, :].rearrange("p (e i) -> p e i", e=2),
                                       ACT.Copy).then_inc(bank_read[6 + n], 1)
                elif kind == "SF":
                    h = step[1]
                    if h:
                        act.wait_ge(fin_stored, 16 * h)
                    for d in range(2):
                        await_full(act, 3 + d, *step)
                        act.activation(fin[:, d, :], bank[3 + d][:, :], ACT.Copy).then_inc(bank_read[3 + d], 1)
                elif kind == "GNA":
                    h = step[1]
                    await_read(act, 5, "FX", h)
                    act.activation(scr[:, 4:8, :], scr[:, 0:4, :], ACT.Square).then_inc(sq_done, 1)
                elif kind == "SS":
                    h = step[1]
                    await_full(act, 5, *step)
                    act.activation(rsb[:, :], bank[5][:, 0:T], ACT.Sqrt, bias=eps[:, 0:1], scale=1.0 / DV)\
                        .then_inc(bank_read[5], 1)
                elif kind == "SH":
                    h = step[1]
                    act.wait_ge(y_done, h + 1)
                    if h >= 2:
                        await_full(act, *tile_use("ro", 8 * (h - 2) + 7))
                    act.activation(ym_hi[:, 4 * (h % 2):4 * (h % 2) + 4, :], scr[:, 0:4, :], ACT.Copy).then_inc(y_hi_done, 1)
                elif kind == "BT":
                    await_full(act, 6, *step)
                elif kind == "QR":
                    await_full(act, 7, "QSS")
                    act.activation(rsq[:, :], bank[7][:, 0:20], ACT.Sqrt, bias=eps[:, 1:2]).then_inc(bank_read[7], 1)
                elif kind == "KP":
                    n = step[1]
                    await_full(act, 4, *step)
                    await_ks(act, n - 2)
                    act.activation(ktc[:, n % 2, 4:8, :], bank[4][:, :].rearrange("p (h k) -> p h k", h=4), ACT.Copy)\
                        .then_inc(bank_read[4], 1)
                elif kind == "KS" and step[1] % 4 == 3:
                    pair = step[1] // 4
                    await_full(act, 5, "PS", pair)
                    act.activation(sst[:, pair, :], bank[5][:, 0:2 * P], ACT.Copy).then_inc(bank_read[5], 1)
                elif kind == "KX":
                    await_full(act, 7, *step)
                    act.activation(mkT[:, 2 * step[1] + 1, :], bank[7][:, 0:T], ACT.Copy).then_inc(bank_read[7], 1)
                elif kind == "SA":
                    p = step[1]
                    act.wait_ge(sa_max, p + 1)
                    act.activation(ps[:, p % 2, :], ps[:, p % 2, :], ACT.Exp, bias=nmxs[:, p:p + 1],
                                   accum_out=dens[:, p:p + 1]).then_inc(sa_exp, 1)
                elif kind == "SB":
                    p = step[1]
                    await_full(act, 6, *step)
                    act.activation(pts[:, p, :], bank[6][:, 0:PAST], ACT.Copy)
                    act.activation(ptn[:, p, :], bank[6][0:TS, PAST:PAST + P], ACT.Copy).then_inc(bank_read[6], 1)
                elif kind == "A":
                    h = step[1]
                    act.wait_ge(a_max, h + 1)
                    for n, cols in enumerate((slice(0, TP), slice(TP, TP + P))):
                        ins = act.activation(pp[:, h % 2, cols], pp[:, h % 2, cols], ACT.Exp, bias=nmx[:, h % 2, n:n + 1],
                                             accum_out=den[:, h % 2, n:n + 1])
                    ins.then_inc(a_exp, 1)
                elif kind == "B":
                    h = step[1]
                    await_full(act, 4, *step)
                    if h >= 2:
                        await_full(act, 6, "C", h - 2)
                    act.activation(pt[:, h % 2, :], bank[4][:, 0:TP + P], ACT.Copy).then_inc(bank_read[4], 1)
                elif kind == "C":
                    h = step[1]
                    await_read(act, 6, *step)
                    if h == 0:
                        await_full(act, *tile_use("mv", 11))
                    act.activation(xn_hi[:, h, 0:TP], yf[:, h % 2, :], ACT.Copy).then_inc(x_hi_done, 1)
                elif kind == "PG":
                    await_read(act, 7, "OSM")
                    await_full(act, *tile_use("mv", 11))
                    act.activation(xn_hi[:, :, TP:T], yfs[:, :, :], ACT.Copy).then_inc(x_hi_done, 1)

        @block.vector
        def _(dve):
            done = Steps(dve, dve_steps)

            def split_lo(c, halves=(0, 1)):
                if c >= nchunks:
                    return
                for n in halves:
                    half_w = slice(CW // 2 * n, CW // 2 * (n + 1))
                    dve.wait_ge(w_hi_done, 2 * c + n + 1)
                    dve.tensor_tensor(w_lo[:, c % 2, half_w], w_raw[:, c % RAW, half_w], w_hi[:, c % 2, half_w].bitcast(F32),
                                      ALU.subtract).then_inc(w_lo_done, 1)

            def mask_keys(s):
                h, b = s // NSEQ, s % NSEQ
                if b == 0:
                    dve.wait_ge(kq_loaded, 128 * (h + 1))
                if s >= 2:
                    await_full(dve, 7, "U", (s - 2) // NSEQ, (s - 2) % NSEQ)
                dve.tensor_scalar(km[:, s % 2, :], kq[:, b // 4, :].bitcast(F32),
                                  cst[:, C_QM + b % 4:C_QM + b % 4 + 1], None, ALU.mult).then_inc(km_done, 1)

            def state_lo(s):
                for d in range(2):
                    dve.wait_ge(st_hi_done, 2 * s + d + 1)
                    dve.tensor_tensor(st_lo[:, d, :], st[:, s % NST, DV * d:DV * d + DV], st_hi[:, d, :].bitcast(F32),
                                      ALU.subtract).then_inc(st_lo_done, 1)

            def normed(kt, col, src):
                dve.scalar_tensor_tensor(scr[:, kt, :], src, wcols[:, col + kt:col + kt + 1], rsb[:, :],
                                         ALU.mult, ALU.mult).then_inc(unsplit_done, 1)

            n_half = [0]

            def upper_half(dst, b):
                n_half[0] += 1
                dve.wait_ge(half_done, n_half[0])
                return dve.tensor_tensor(dst, bank[b][0:TS, 0:256], half[:, :], ALU.add)

            nk = 0
            for step in steps:
                kind = step[0]
                if kind == "CHUNK":
                    split_lo(step[1] + 1)
                elif kind == "X":
                    dve.wait_ge(roots_done, 1)
                    done(dve.reciprocal(rms[:, 0:2], rms[:, 0:2]))
                    dve.wait_ge(roots_done, 2)
                    done(dve.reciprocal(rms[0:TS, 2:3], rms[0:TS, 2:3]))
                    done.wait()
                    dve.wait_ge(const_loaded, 16 * 6)
                    for t, (c0, m) in enumerate(TOK):
                        ins = dve.tensor_scalar(diag[0:m, t, 0:m], ident[0:m, 0:m], rms[0:m, t:t + 1], None, ALU.mult)
                    ins.then_inc(diag_done, 1)
                    await_full(dve, 0, "X", 0)
                    done(dve.tensor_copy(wcols[:, 0:41], bank[0][:, 384:425]))
                elif kind == "NORM":
                    dve.wait_ge(rms_done, 1)
                    for t, (c0, m) in enumerate(TOK):
                        done(dve.tensor_copy(rsb[:, c0:c0 + m], bank[1 + t][:, 384:384 + m]))
                    done.wait()
                    split_lo(0, (0,))
                    for kt in range(KT + 1):
                        if kt < KT:
                            await_full(dve, kt, "X", kt)
                            normed(kt, W_RET, bank[kt][:, 0:T])
                        if kt == 2:
                            split_lo(0, (1,))
                        if kt:
                            dve.wait_ge(x_hi_done, kt)
                            dve.tensor_tensor(xn_lo[:, kt - 1, :], scr[:, kt - 1, :], xn_hi[:, kt - 1, 0:T].bitcast(F32),
                                              ALU.subtract).then_inc(x_lo_done, 1)
                elif kind == "W":
                    kt = step[1]
                    dve.wait_ge(x_hi_done, KT + kt + 1)
                    dve.scalar_tensor_tensor(ym_lo[:, kt, :], xT[:, kt, :], wcols[:, W_MOBA + kt:W_MOBA + kt + 1],
                                             ym_hi[:, kt, :].bitcast(F32), ALU.mult, ALU.subtract).then_inc(x_lo_done, 1)
                elif kind == "RMS":
                    await_read(dve, 7, "NORM", 1)
                    done(dve.reciprocal(rsb[:, :], rsb[:, :]))
                    done.wait()
                elif kind == "NB":
                    kt = step[1]
                    if kt < KT:
                        normed(kt, W_KV, xT[:, kt, :])
                    if kt:
                        dve.wait_ge(x_hi_done, 2 * KT + kt)
                        dve.tensor_tensor(xn_lo[:, kt - 1, :], scr[:, kt - 1, :], xn_hi[:, kt - 1, 0:T].bitcast(F32),
                                          ALU.subtract).then_inc(x_lo_done, 1)
                elif kind == "ME":
                    head = step[1]
                    b = tile_use("mq", head)[0]
                    await_full(dve, *tile_use("mq", head))
                    if head >= 2:
                        dve.wait_ge(q_done, head - 1)
                    dve.tensor_tensor(ps[:, head % 2, :], bank[b][:, 0:T], rsb[:, :], ALU.mult).then_inc(bank_read[b], 1)
                elif kind == "TILE":
                    c, i, b = step[1:]
                    what, h, part = chunks[c]
                    if what == "ro":
                        n = 4 * part + i
                        await_full(dve, b, *step[:3])
                        if h:
                            await_read(dve, *tile_use("ro", 8 * (h - 1) + n))
                        dve.tensor_tensor(xT[:, n, :], xT[:, n, :], bank[b][:, 0:T], ALU.add).then_inc(bank_read[b], 1)
                    elif what == "rv" and i == 2:
                        if h:
                            await_full(dve, 5, "OSI", h - 1)
                            dve.wait_ge(vs_lo_done, 2 * h)
                        upper_half(vs[:, 256 * part:256 * part + 256], b).then_inc(bank_read[b], 1)
                    elif what == "mv" and i == 2:
                        upper_half(mvs[:, 256 * h:256 * h + 256], b).then_inc(bank_read[b], 1)
                    elif what == "mg":
                        await_full(dve, b, *step[:3])
                        dve.tensor_tensor(scr[:, 2 * h + i, :], bank[b][:, 0:T], rsb[:, :], ALU.mult).then_inc(bank_read[b], 1)
                    elif what == "mk":
                        m = TOK[i][1]
                        src = bank[b]
                        if i == 2:
                            src = half
                            upper_half(half[:, :], b).then_inc(sum_done, 1)
                        dve.wait_ge(kss_done, nk + 1)
                        done(dve.reciprocal(kss[0:m, nk % 2, :], kss[0:m, nk % 2, :]))
                        done.wait()
                        if h >= 2:
                            dve.wait_ge(rows_stored[h % 2], 48)
                            await_full(dve, 7, "KX", h - 2)
                        for d in range(2):
                            ins = dve.scalar_tensor_tensor(rows[0:m, h % 2, i, P * d:P * d + P], src[0:m, P * d:P * d + P],
                                                           kss[0:m, nk % 2, d:d + 1], knw[0:m, :], ALU.mult, ALU.mult)
                        ins.then_inc(bank_read[b], 1)
                        nk += 1
                    elif what == "mo" and i == 2:
                        dve.wait_ge(rows_stored[h % 2], 48 * (2 + h // 2))
                        upper_half(rows[0:TS, h % 2, i, :], b).then_inc(bank_read[b], 1)
                    elif what == "mo" and i == 1:
                        await_full(dve, b, *step[:3])
                        dve.wait_ge(rows_stored[h % 2], 48 * (2 + h // 2))
                        dve.tensor_copy(rows[0:TOK[i][1], h % 2, i, :], bank[b][0:TOK[i][1], 0:256]).then_inc(bank_read[b], 1)
                elif kind == "SC":
                    h = step[1]
                    await_full(dve, 5, *step)
                    if h == 0:
                        dve.wait_ge(cst_loaded, 16)
                    else:
                        await_full(dve, 7, "OP", h - 1)
                        await_full(dve, 5, "OSI", h - 1)
                    dve.wait_ge(dt_loaded, 16 * (h + 1))
                    dve.tensor_tensor(sT[:, 0:TP], bank[5][:, 0:TP], dt[:, :], ALU.mult)
                    dve.tensor_tensor(sT[:, TP:TP + P], bank[5][:, TP:TP + P], dt[:, 0:P], ALU.mult)
                    dve.tensor_tensor(s2[:, :], bank[5][0:TS, TP + P:TP + P + TS],
                                      cst[0:TS, C_DS + TS * h:C_DS + TS * h + TS], ALU.mult).then_inc(bank_read[5], 1)
                elif kind == "ENDCHUNK" and chunks[step[1]][0] == "rg" and chunks[step[1]][2] == 1:
                    if chunks[step[1]][1] == 0:
                        state_lo(0)
                    mask_keys(NSEQ * chunks[step[1]][1])
                elif kind == "U":
                    h, b = step[1:]
                    s = NSEQ * h + b
                    if b < NSEQ - 1:
                        mask_keys(s + 1)
                    if s + 1 < RH * NSEQ:
                        state_lo(s + 1)
                    for d in range(2):
                        await_full(dve, 6 + d, *step)
                        state = st[:, s % NST, DV * d:DV * d + DV]
                        dve.scalar_tensor_tensor(state, state, math.exp(NEW * LOG_DECAY[h]), bank[6 + d][:, :],
                                                 ALU.mult, ALU.add).then_inc(bank_read[6 + d], 1)
                elif kind == "FX":
                    await_full(dve, 5, *step)
                    new = scr[:, 0:4, TP:T]
                    dve.tensor_tensor(new, new, bank[5][:, 0:4 * TS].rearrange("p (e i) -> p e i", e=4), ALU.add)\
                        .then_inc(bank_read[5], 1)
                elif kind == "SR":
                    await_read(dve, 5, "SS", step[1])
                    done(dve.reciprocal(rsb[:, :], rsb[:, :]))
                    done.wait()
                elif kind == "SG":
                    h = step[1]
                    for i in range(4 * h, 4 * h + 4):
                        await_read(dve, *tile_use("rg", i))
                    dve.wait_ge(sq_done, h + 1)
                    for e in range(4):
                        w = wcols[:, W_GN + 4 * h + e:W_GN + 4 * h + e + 1]
                        ins = dve.scalar_tensor_tensor(scr[:, e, :], scr[:, e, :], w, gs[:, e, :], ALU.mult, ALU.mult)
                    ins.then_inc(gated_done, 1)
                elif kind == "SM":
                    dve.wait_ge(gated_done, step[1] + 1)
                    dve.tensor_tensor(scr[:, 0:4, :], scr[:, 0:4, :],
                                      rsb[:, :].rearrange("p (o t) -> p o t", o=1).broadcast_to((P, 4, T)), ALU.mult)\
                        .then_inc(y_done, 1)
                elif kind == "SH":
                    h = step[1]
                    dve.wait_ge(y_hi_done, h + 1)
                    dst = slice(4 * (h % 2), 4 * (h % 2) + 4)
                    dve.tensor_tensor(ym_lo[:, dst, :], scr[:, 0:4, :], ym_hi[:, dst, :].bitcast(F32), ALU.subtract)\
                        .then_inc(y_lo_done, 1)
                elif kind == "BT":
                    await_full(dve, 6, *step)
                    done(dve.memset(line[:, :], MASKED))
                    done.wait()
                    dve.tensor_copy(line[:, 0:FAR + 1], bank[6][0:MH, 0:FAR + 1]).then_inc(bank_read[6], 1)
                elif kind == "QR":
                    await_read(dve, 7, "QSS")
                    done(dve.reciprocal(rsq[:, :], rsq[:, :]))
                    done.wait()
                elif kind == "KP":
                    n = step[1]
                    await_full(dve, 3, *step)
                    await_ks(dve, n - 2)
                    dve.tensor_copy(ktc[:, n % 2, 0:4, :], bank[3][:, :].rearrange("p (h k) -> p h k", h=4))\
                        .then_inc(bank_read[3], 1)
                elif kind == "KX":
                    await_full(dve, 6, *step)
                    dve.tensor_copy(mkT[:, 2 * step[1], :], bank[6][:, 0:T]).then_inc(bank_read[6], 1)
                elif kind == "SN":
                    await_full(dve, 6, *step)
                    dve.tensor_copy(sstn[:, :], bank[6][0:TS, :]).then_inc(bank_read[6], 1)
                elif kind == "SA":
                    p = step[1]
                    if p == 0:
                        dve.wait_ge(bias_loaded, 16 * 11)
                    await_full(dve, 5, *step)
                    if p >= 2:
                        await_full(dve, 6, "SB", p - 2)
                    r = rsq[:, 16 + p:17 + p]
                    dve.scalar_tensor_tensor(ps[:, p % 2, 0:PAST], bank[5][:, 0:PAST], r, bs[:, :], ALU.mult, ALU.add)
                    dve.scalar_tensor_tensor(ps[:, p % 2, PAST:T], bank[5][:, PAST:T], r, bn[:, p, :], ALU.mult, ALU.add)\
                        .then_inc(bank_read[5], 1)
                    await_read(dve, 5, *step)
                    dve.tensor_reduce(nmxs[:, p:p + 1], ps[:, p % 2, :], AX.X, ALU.max, negate=True).then_inc(sa_max, 1)
                    dve.wait_ge(sa_exp, p + 1)
                    done(dve.reciprocal(dens[:, p:p + 1], dens[:, p:p + 1]))
                    done.wait()
                    dve.tensor_scalar(ps[:, p % 2, :], ps[:, p % 2, :], dens[:, p:p + 1], None, ALU.mult).then_inc(sa_done, 1)
                elif kind == "A":
                    h = step[1]
                    await_full(dve, 3, *step)
                    if h >= 2:
                        await_full(dve, 4, "B", h - 2)
                    dve.scalar_tensor_tensor(pp[:, h % 2, 0:TP], bank[3][:, 0:TP], rsq[:, 2 * h + 1:2 * h + 2], tb[:, h, :],
                                             ALU.mult, ALU.add)
                    dve.scalar_tensor_tensor(pp[:, h % 2, TP:TP + P], bank[3][:, TP:TP + P], rsq[:, 2 * h:2 * h + 1],
                                             tb[:, h, P:TP], ALU.mult, ALU.add).then_inc(bank_read[3], 1)
                    await_read(dve, 3, *step)
                    dve.tensor_reduce(nmx[:, h % 2, 0:1], pp[:, h % 2, 0:TP], AX.X, ALU.max, negate=True)
                    dve.tensor_reduce(nmx[:, h % 2, 1:2], pp[:, h % 2, TP:TP + P], AX.X, ALU.max, negate=True).then_inc(a_max, 1)
                    dve.wait_ge(a_exp, h + 1)
                    done(dve.reciprocal(den[:, h % 2, :], den[:, h % 2, :]))
                    done.wait()
                    dve.tensor_scalar(pp[:, h % 2, 0:TP], pp[:, h % 2, 0:TP], den[:, h % 2, 0:1], None, ALU.mult)
                    dve.tensor_scalar(pp[:, h % 2, TP:TP + P], pp[:, h % 2, TP:TP + P], den[:, h % 2, 1:2], None, ALU.mult)\
                        .then_inc(a_done, 1)
                elif kind == "C":
                    h = step[1]
                    await_full(dve, 6, *step)
                    dve.wait_ge(gate_done, h + 1)
                    dve.tensor_tensor(yf[:, h % 2, :], bank[6][:, 0:TP], scr[:, h, 0:TP], ALU.mult).then_inc(bank_read[6], 1)
                    dve.wait_ge(x_hi_done, 24 + h + 1)
                    dve.tensor_tensor(xn_lo[:, h, 0:TP], yf[:, h % 2, :], xn_hi[:, h, 0:TP].bitcast(F32), ALU.subtract)\
                        .then_inc(x_lo_done, 1)
                elif kind == "PG":
                    await_full(dve, 7, "OSM")
                    dve.wait_ge(gate_done, MH)
                    dve.tensor_tensor(yfs[:, :, :], bank[7][:, :].rearrange("p (h i) -> p h i", h=MH), scr[:, :, TP:T],
                                      ALU.mult).then_inc(bank_read[7], 1)
                    dve.wait_ge(x_hi_done, 24 + MH + 1)
                    dve.tensor_tensor(xn_lo[:, :, TP:T], yfs[:, :, :], xn_hi[:, :, TP:T].bitcast(F32), ALU.subtract)\
                        .then_inc(x_lo_done, 1)

        @block.gpsimd
        def _(pool):
            done = Steps(pool, pool_steps)
            done(pool.memset(eps[:, 0:1], EPS))
            done(pool.memset(qdm[:, :, :, :].bitcast(F32), 0.0))
            done.wait()
            pool.memset(eps[:, 1:2], EPS * HD).then_inc(eps_done, 1)
            cos, sin = cst[:, C_COS:C_COS + T], cst[:, C_SIN:C_SIN + T]
            for step in steps:
                kind = step[0]
                if kind == "TILE" and chunks[step[1]][0] in ("rq", "rk") and step[2] == 1:
                    c, i, b = step[1:]
                    what, h, _ = chunks[c]
                    qk = int(what == "rk")
                    if h == 0 and qk == 0:
                        pool.wait_ge(cst_loaded, 16)
                    for n in range(2):
                        await_read(pool, *tile_use(what, 2 * h + n))
                    if h:
                        await_full(pool, 5, "SC", h - 1)
                    if h and not qk:
                        pool.wait_ge(qd_hi_done, h)
                    x1, x2, dst = raw_qk[:, qk, 0, :], raw_qk[:, qk, 1, :], (qT, kT)[qk]
                    if done.n > 1:
                        done.wait()
                    for n, (x, tab, to) in enumerate(((x1, cos, rt[:, 0, :]), (x2, sin, rt[:, 1, :]), (x1, sin, x1), (x2, cos, x2))):
                        if n == 2:
                            done.wait()
                        done(pool.tensor_tensor(to, x, tab, ALU.mult))
                    done.wait()
                    done(pool.tensor_tensor(dst[:, 0, :], rt[:, 0, :], rt[:, 1, :], ALU.subtract))
                    ins = pool.tensor_tensor(dst[:, 1, :], x1, x2, ALU.add)
                    if not qk:
                        done(ins)
                        done.wait()
                        dec = cst[:, C_QD + TS * h:C_QD + TS * h + TS]
                        done(pool.tensor_tensor(qd[:, 0, :], qT[:, 0, TP:T], dec, ALU.mult))
                        ins = pool.tensor_tensor(qd[:, 1, :], qT[:, 1, TP:T], dec, ALU.mult)
                    ins.then_inc(rot_done, 1)
                    pool.wait_ge(rot_done, 2 * h + qk + 1)
                elif kind == "TILE" and chunks[step[1]][0] == "rv" and step[2] == 2:
                    h, part = chunks[step[1]][1:]
                    cols = slice(256 * part, 256 * part + 256)
                    pool.wait_ge(vs_hi_done, 2 * h + part + 1)
                    pool.tensor_tensor(vs_lo[:, cols], vs[:, cols], vs_hi[:, cols].bitcast(F32), ALU.subtract)\
                        .then_inc(vs_lo_done, 1)
                elif kind == "KT":
                    pool.wait_ge(ks_hi_done, step[1] + 1)
                    pool.tensor_tensor(ks_lo[:, :], ks[:, :], ks_hi[:, :].bitcast(F32), ALU.subtract).then_inc(ks_lo_done, 1)
                    pool.wait_ge(qd_hi_done, step[1] + 1)
                    for j in range(4):
                        ins = pool.tensor_tensor(qdm_at(j, 1), qd_at(j), qdm_at(j, 0).bitcast(F32), ALU.subtract)
                    ins.then_inc(qd_lo_done, 1)
                elif kind == "BT":
                    await_full(pool, 6, *step)
                    pool.memset(bn[:, :, :], MASKED).then_inc(bn_masked, 1)


_OUTS = [("y_prompt", (1, TP, D)), ("y_sample", (NSEQ, NEW, D)),
         ("ret_state_prompt", (1, 1, RH, DK, DV)), ("ret_state_sample", (1, NSEQ, RH, DK, DV)),
         ("k_prompt", (1, TP, MH, HD)), ("v_prompt", (1, TP, MH, HD)),
         ("k_sample", (NSEQ, NEW, MH, HD)), ("v_sample", (NSEQ, NEW, MH, HD))]


def kernel(**inputs):
    import concourse.bacc as bacc
    from concourse.bass_utils import run_bass_kernel_spmd

    nc = bacc.Bacc("TRN2", target_bir_lowering=False, num_devices=1)
    arrays, aps = {}, {}
    given = {name: np.ascontiguousarray(v) for name, v in inputs.items()}
    given["c_ret"], given["c_eye"], given["c_hot"] = shape_constants()
    for name, v in given.items():
        arrays[f"in_{name}"] = v
        aps[name] = nc.dram_tensor(f"in_{name}", v.shape, mybir.dt.from_np(v.dtype), kind="ExternalInput").ap()
    for name, shape in _OUTS:
        aps[name] = nc.dram_tensor(f"out_{name}", shape, F32, kind="ExternalOutput").ap()
    build(nc, aps)
    r = run_bass_kernel_spmd(nc, [arrays], core_ids=[0])
    return tuple(r.results[0][f"out_{name}"] for name, _ in _OUTS)
```
